# Optimizing a Trainium2 kernel written in Bass

```python
import jax, jax.numpy as jnp
from jax import lax
import numpy as np

D_MODEL = 1024
BATCH = 1
SEQ = 512
DEPTH = 1

GRID_W = 64
HEAD_DIM = 64
NA_HEADS = 8
NA_WIN_ROWS = 8
NA_WIN_COLS = 16
GQA_HEADS = 8
GQA_KV_HEADS = 2
ROPE_BASE = 10000.0
Q_BLOCK = 128
N_EXPERTS = 16
EC_CAPACITY_FACTOR = 2
EXPERT_FF = 2048
N_BRANCHES = 2
EPS = 1e-6

NA_WIDTH = NA_HEADS * HEAD_DIM
GQA_WIDTH = GQA_HEADS * HEAD_DIM
GQA_KV_WIDTH = GQA_KV_HEADS * HEAD_DIM
IN_WIDTH = 3 * NA_WIDTH + GQA_WIDTH + 2 * GQA_KV_WIDTH + N_BRANCHES * D_MODEL

kernel_name = "hybrid_na_gqa_ec_moe_block"

def rmsnorm(x, g):
    x32 = x.astype(jnp.float32)
    y = x32 * lax.rsqrt(jnp.mean(x32 * x32, axis=-1, keepdims=True) + EPS)
    return y.astype(x.dtype) * g

def neighbourhood_attention(q, k, v, rpb):
    B, T, H, hd = q.shape
    rows = T // GRID_W
    kh = min(NA_WIN_ROWS, rows)
    kw = NA_WIN_COLS
    qg = q.reshape(B, rows, GRID_W, H, hd)
    kg = k.reshape(B, rows, GRID_W, H, hd)
    vg = v.reshape(B, rows, GRID_W, H, hd)
    cols = jnp.arange(GRID_W)
    col_start = jnp.clip(cols - kw // 2, 0, GRID_W - kw)
    col_idx = col_start[:, None] + jnp.arange(kw)[None, :]
    dc = col_idx - cols[:, None] + (NA_WIN_COLS - 1)
    scale = hd ** -0.5

    def one_row(r):
        r_start = jnp.clip(r - kh // 2, 0, rows - kh)
        k_band = lax.dynamic_slice_in_dim(kg, r_start, kh, axis=1)
        v_band = lax.dynamic_slice_in_dim(vg, r_start, kh, axis=1)
        k_nb = k_band[:, :, col_idx]
        v_nb = v_band[:, :, col_idx]
        q_r = lax.dynamic_index_in_dim(qg, r, axis=1, keepdims=False)
        dr = r_start + jnp.arange(kh) - r + (NA_WIN_ROWS - 1)
        bias = rpb[:, dr][:, :, dc]
        bias = bias.transpose(0, 2, 1, 3).astype(jnp.float32)
        s = jnp.einsum('bqhd,brqjhd->bhqrj', q_r, k_nb).astype(jnp.float32) * scale + bias[None]
        p = jax.nn.softmax(s.reshape(B, H, GRID_W, kh * kw), axis=-1)
        p = p.reshape(B, H, GRID_W, kh, kw).astype(v.dtype)
        return jnp.einsum('bhqrj,brqjhd->bqhd', p, v_nb)

    out = lax.map(one_row, jnp.arange(rows))
    return out.transpose(1, 0, 2, 3, 4).reshape(B, T, H * hd)

def axial_rope_tables(T):
    t = jnp.arange(T)
    row = (t // GRID_W).astype(jnp.float32)
    col = (t % GRID_W).astype(jnp.float32)
    half = HEAD_DIM // 2
    inv_freq = ROPE_BASE ** (-jnp.arange(0, half, 2, dtype=jnp.float32) / half)
    ang = jnp.concatenate([row[:, None] * inv_freq[None], col[:, None] * inv_freq[None]], axis=-1)
    return jnp.cos(ang), jnp.sin(ang)

def apply_rope(x, cos, sin):
    xp = x.astype(jnp.float32).reshape(*x.shape[:-1], HEAD_DIM // 2, 2)
    x0, x1 = xp[..., 0], xp[..., 1]
    c = cos[None, :, None, :]
    s = sin[None, :, None, :]
    out = jnp.stack([x0 * c - x1 * s, x0 * s + x1 * c], axis=-1).reshape(x.shape)
    return out.astype(x.dtype)

def gqa_attention(q, k, v):
    B, T, Hq, hd = q.shape
    G = Hq // GQA_KV_HEADS
    nblk = T // Q_BLOCK
    qb = q.reshape(B, nblk, Q_BLOCK, GQA_KV_HEADS, G, hd).transpose(1, 0, 2, 3, 4, 5)
    scale = hd ** -0.5

    def one_block(q_blk):
        s = jnp.einsum('bqkgd,bskd->bkgqs', q_blk, k).astype(jnp.float32) * scale
        p = jax.nn.softmax(s, axis=-1).astype(v.dtype)
        return jnp.einsum('bkgqs,bskd->bqkgd', p, v)

    out = lax.map(one_block, qb)
    return out.transpose(1, 0, 2, 3, 4, 5).reshape(B, T, Hq * hd)

def expert_choice_ffn(h, w_router, w_gate, w_up, w_down):
    B, T, D = h.shape
    cap = EC_CAPACITY_FACTOR * T // N_EXPERTS
    logits = jnp.einsum('btd,de->bte', h, w_router).astype(jnp.float32)
    aff = jax.nn.softmax(logits, axis=-1)
    g, idx = lax.top_k(aff.transpose(0, 2, 1), cap)
    xin = jax.vmap(lambda hb, ib: hb[ib])(h, idx)
    a = jnp.einsum('becd,edf->becf', xin, w_gate)
    u = jnp.einsum('becd,edf->becf', xin, w_up)
    y = jnp.einsum('becf,efd->becd', jax.nn.silu(a) * u, w_down)
    y = y * g[..., None].astype(y.dtype)
    flat = (jnp.arange(B)[:, None, None] * T + idx).reshape(-1)
    out = jax.ops.segment_sum(y.reshape(-1, D), flat, num_segments=B * T)
    return out.reshape(B, T, D).astype(h.dtype)

def setup_inputs(seed: int = 0) -> dict:
    key = jax.random.key(seed)
    ks = jax.random.split(key, 20)
    f32 = jnp.float32
    D, L, F, E = D_MODEL, DEPTH, EXPERT_FF, N_EXPERTS
    nrm = lambda k, shape, s: jax.random.normal(k, shape, f32) * s
    return {
        "x": nrm(ks[0], (BATCH, SEQ, D), 1.0),
        "c": nrm(ks[1], (BATCH, D), 1.0),
        "w_ada": nrm(ks[2], (L, D, 6 * D), 0.5 * D ** -0.5),
        "b_ada": nrm(ks[3], (L, 6 * D), 0.02),
        "norm1_g": 1.0 + nrm(ks[4], (L, D), 0.02),
        "w_in": nrm(ks[5], (L, D, IN_WIDTH), D ** -0.5),
        "q_norm_g": 1.0 + nrm(ks[6], (L, HEAD_DIM), 0.02),
        "k_norm_g": 1.0 + nrm(ks[7], (L, HEAD_DIM), 0.02),
        "na_rpb": nrm(ks[8], (L, NA_HEADS, 2 * NA_WIN_ROWS - 1, 2 * NA_WIN_COLS - 1), 0.1),
        "w_branch_na": nrm(ks[9], (L, NA_WIDTH, D), NA_WIDTH ** -0.5),
        "w_branch_gqa": nrm(ks[10], (L, GQA_WIDTH, D), GQA_WIDTH ** -0.5),
        "w_out": nrm(ks[11], (L, D, D), D ** -0.5),
        "norm2_g": 1.0 + nrm(ks[12], (L, D), 0.02),
        "w_router": nrm(ks[13], (L, D, E), D ** -0.5),
        "w_exp_gate": nrm(ks[14], (L, E, D, F), D ** -0.5),
        "w_exp_up": nrm(ks[15], (L, E, D, F), D ** -0.5),
        "w_exp_down": nrm(ks[16], (L, E, F, D), F ** -0.5),
        "final_g": 1.0 + nrm(ks[17], (D,), 0.02),
    }

def reference(x, c, w_ada, b_ada, norm1_g, w_in, q_norm_g, k_norm_g, na_rpb, w_branch_na, w_branch_gqa,
              w_out, norm2_g, w_router, w_exp_gate, w_exp_up, w_exp_down, final_g):
    B, T, D = x.shape
    cos, sin = axial_rope_tables(T)
    split_points = np.cumsum([NA_WIDTH, NA_WIDTH, NA_WIDTH, GQA_WIDTH, GQA_KV_WIDTH, GQA_KV_WIDTH]).tolist()
    for l in range(DEPTH):
        mod = jnp.einsum('bd,de->be', jax.nn.silu(c), w_ada[l]) + b_ada[l]
        shift1, scale1, gate1, shift2, scale2, gate2 = [m[:, None, :] for m in jnp.split(mod, 6, axis=-1)]

        h = rmsnorm(x, norm1_g[l]) * (1.0 + scale1) + shift1
        proj = jnp.einsum('btd,de->bte', h, w_in[l])
        q_na, k_na, v_na, q_g, k_g, v_g, gate_logits = jnp.split(proj, split_points, axis=-1)

        heads = lambda t, n: t.reshape(B, T, n, HEAD_DIM)
        y_na = neighbourhood_attention(heads(q_na, NA_HEADS), heads(k_na, NA_HEADS),
                                       heads(v_na, NA_HEADS), na_rpb[l])

        qg = apply_rope(rmsnorm(heads(q_g, GQA_HEADS), q_norm_g[l]), cos, sin)
        kg = apply_rope(rmsnorm(heads(k_g, GQA_KV_HEADS), k_norm_g[l]), cos, sin)
        y_gqa = gqa_attention(qg, kg, heads(v_g, GQA_KV_HEADS))

        gates = jax.nn.sigmoid(gate_logits.astype(jnp.float32)).astype(x.dtype)
        g_na, g_gqa = jnp.split(gates, N_BRANCHES, axis=-1)
        merged = (g_na * jnp.einsum('btk,kd->btd', y_na, w_branch_na[l])
                  + g_gqa * jnp.einsum('btk,kd->btd', y_gqa, w_branch_gqa[l]))
        x = x + gate1 * jnp.einsum('btd,de->bte', merged, w_out[l])

        h2 = rmsnorm(x, norm2_g[l]) * (1.0 + scale2) + shift2
        x = x + gate2 * expert_choice_ffn(h2, w_router[l], w_exp_gate[l], w_exp_up[l], w_exp_down[l])
    return rmsnorm(x, final_g)


_drawn_inputs = setup_inputs


def setup_inputs(seed=0):
    import zlib

    import numpy as np

    out = dict(_drawn_inputs(seed))
    spreads = {}
    factors = {'b_ada': 5.335,
     'norm1_g': 8.0,
     'q_norm_g': 8.0,
     'k_norm_g': 8.0,
     'na_rpb': 8.0,
     'norm2_g': 8.0,
     'final_g': 2.876}
    for name, (base, spread) in spreads.items():
        noise = np.random.default_rng([zlib.crc32(name.encode()), seed]).standard_normal(out[name].shape)
        drawn = base * np.exp(spread * noise) if base else spread * noise
        out[name] = __import__('jax').numpy.asarray(drawn.astype(out[name].dtype))
    for name, factor in factors.items():
        out[name] = (out[name] * factor).astype(out[name].dtype)
    return out
```

```python
import concourse.bass as bass
from concourse import mybir
from contextlib import ExitStack


def encoder_block(nc, x, c, w_ada, b_ada, norm1_g, w_in, q_norm_g, k_norm_g, na_rpb, w_branch_na, w_branch_gqa,
                  w_out, norm2_g, w_router, w_exp_gate, w_exp_up, w_exp_down, final_g, consts, out):
    f32 = mybir.dt.float32
    ALU = mybir.AluOpType
    ACT = mybir.ActivationFunctionType
    X = mybir.AxisListType.X

    P = 128
    T, D = x.shape[1], x.shape[2]
    COLS = 64
    ROWS = T // COLS
    NT = T // P
    KD = D // P
    H, HD = 8, 64
    NH = H * HD
    E = w_router.shape[1]
    F = w_exp_gate.shape[2]
    CAP = 2 * T // E
    EPS = 1e-6
    QS = HD ** -0.5
    B = 512

    TILE = 4096
    RING = 6
    FRONT_SLOTS = 3
    N_FRONT = 13
    slot_of = lambda m: m % FRONT_SLOTS if m < 12 else 3
    uses_of = lambda m: m // FRONT_SLOTS + 1 if m < 12 else 1
    FRONT_USES = [sum(slot_of(m) == s for m in range(N_FRONT)) for s in range(RING)]
    ET = 12
    E_ORDER = [4, 5, 0, 1, 2, 3]
    eslot = lambda i: E_ORDER[i % RING]
    NADA = 12

    B_X = 0
    B_NA = B_X + KD
    B_YN = B_NA + 2 * 16
    B_K = B_YN + 4
    B_Q = B_K + 1
    B_GQ = B_Q + 4
    B_YG = B_GQ + 2 * 16
    B_X2 = B_YG + 4
    B_AFF = B_X2 + KD
    B_SLOT = B_AFF + 1
    N_BATCH = B_SLOT + 1

    G_Q, G_K, G_V, G_KV, G_QG, G_GATE = 0, 4, 8, 12, 16, 20
    N_PROJ = 36
    proj_bank = lambda n: [0, 1, 3, 7][n % 4] if n < G_KV else 7
    proj_tile = lambda n: n // 4 if n < 16 else 4 if n < 20 else 5 + (n - 20) // 4

    proj_end = lambda m: 4 * (m + 1)

    NAJ = [(1, 64, 256, 0, 3, 0), (2, 192, 256, 128, 3, 0), (3, 320, 192, 256, 2, 2), (0, 0, 256, 0, 2, 1)]

    ctx = ExitStack()
    with ctx:
        def sb(name, shape):
            return ctx.enter_context(nc.sbuf_tensor(name, shape, f32))

        def sem(name):
            return ctx.enter_context(nc.semaphore(name))

        ring = sb("ring", [P, RING * TILE])
        slot = lambda s: ring[:, s * TILE:(s + 1) * TILE]
        xs = sb("x_sb", [P, NT, D])
        ht = sb("ht", [P, KD, T])
        sig = sb("sig", [P, 2 * KD, T])
        vy = sb("vy", [P, NT, NH])
        qy = sb("qy", [P, 2, NT, NH])
        bias = sb("bias", [P, H, 32, ROWS])
        bm = sb("bm", [P, 2, 2, 256])
        cst = sb("cst", [P, consts.shape[1]])
        gains = sb("gains", [P, 2, HD])
        wr = sb("wr", [P, KD, E])
        vecs = sb("vecs", [24, P])
        col = sb("col", [P, 7, KD])
        stat = sb("stat", [P, 128])
        rsum = sb("rsum", [P, 64])
        nmax = sb("nmax", [P, 64])
        rinv = sb("rinv", [P, 64])
        aff = sb("aff", [P, NT, E])
        slots = sb("slots", [P, NT, E + 1])
        ones = sb("ones", [P, P])
        nhalf = sb("nhalf", [P, 8])
        grow = sb("grow", [P, 512])

        ident = cst[:, 0:P]
        iota = cst[:, P:2 * P]
        cos = cst[:, 2 * P:3 * P].rearrange("p (j f) -> p j f", j=NT)
        sin = cst[:, 3 * P:4 * P].rearrange("p (j f) -> p j f", j=NT)
        mask = cst[:, 4 * P:4 * P + 768].rearrange("p (v k) -> p v k", v=3)
        cT, n1c, n2c, a1, s1, a2, s2 = (col[:, i, :] for i in range(7))

        r3, r4, r5 = slot(3), slot(4), slot(5)
        qk = r3.rearrange("p (b t) -> p b t", b=8)
        pb = r4[:, 0:2048].rearrange("p (u k) -> p u k", u=4)
        ssb = r4[:, 2048:2560].rearrange("p (u k) -> p u k", u=2)
        ptb = r4[:, 2560:3584].rearrange("p (u k) -> p u k", u=2)
        adab = r4[:, 2560:4096].rearrange("p (g n) -> p g n", g=3)
        qt = r5[:, 0:2048].rearrange("p (b t) -> p b t", b=4)
        kvg = r5[:, 2048:3072].rearrange("p (j n) -> p j n", j=NT)
        kt = r5[:, 3072:3584]
        sigf = sig[:, :, :].rearrange("p b t -> p (b t)")
        ada_slot = lambda m: sigf[:, (m % 2) * TILE:(m % 2 + 1) * TILE].rearrange("p (k n) -> p k n", k=2)
        qyf = qy[:, :, :, :].rearrange("p a j n -> p (a j n)")
        xh = qyf.rearrange("p (j d) -> p j d", j=NT)
        adar = vy[:, 0:2, :]
        braw = qyf[:, 0:2048].rearrange("p (r h c) -> p r h c", h=H, r=ROWS)
        rt = sigf[:, 7168:8192]
        ytok = qy[:, 1, :, :]
        ytn = vy
        ytg = qy[:, 0, :, :]
        biasf = bias[:, :, :, :].rearrange("p h c r -> p (h c r)")
        gate1 = biasf[:, 0:D]
        fing = biasf[:, D:2 * D]
        gate2 = bm[:, 0, :, :].rearrange("p a k -> p (a k)")
        xh2 = sigf[:, 0:4096].rearrange("p (j d) -> p j d", j=NT)
        h2t = sigf[:, 4096:8192].rearrange("p (k t) -> p k t", k=KD)
        work = ht[0:E, 0, :]
        cum = ht[0:E, 1, :]
        sel = ht[0:E, 2, :]
        slot_e = ht[0:E, 3, :]
        top8 = ht[0:E, 4, 0:64]
        onesr = ht[0:E, 5, :]
        ef = sigf[:, 4096:8192]
        act = ef[:, 0:1024].rearrange("p (g n) -> p g n", g=2)
        silu = ef[:, 1024:2048].rearrange("p (g n) -> p g n", g=2)
        actT = ef[:, 2048:3072].rearrange("p (f s) -> p f s", f=16)
        ysb = ef[:, 3072:3584]
        xin = ef[:, 3584:4096]
        vf = vy[:, :, :].rearrange("p j n -> p (j n)")
        xinT = vf[:, 0:512].rearrange("p (k s) -> p k s", k=KD)
        pick = vf[:, 512:768].rearrange("p (j s) -> p j s", j=NT)
        give = vf[:, 768:1280].rearrange("p (j s) -> p j s", j=NT)
        giveT = vf[:, 1280:1792]

        ps = ctx.enter_context(nc.psum_tensor("ps", [P, 8, B], f32))

        s_const, s_x, s_vec, s_rpb, s_small, s_fing = map(sem, ("const_in", "x_in", "vec_in", "rpb_in", "small_in", "fing_in"))
        s_adab = sem("adab_in")
        s_w = [sem(f"w_in{s}") for s in range(RING)]
        s_ada = [sem(f"ada_in{s}") for s in range(2)]
        s_wused = sem("w_used")
        s_adaused = sem("ada_used")
        s_ones = sem("ones_ready")
        s_xh = sem("xh_ready")
        s_tdone = sem("t_done")
        s_tout = [sem("t_out_dve"), sem("t_out_act")]
        s_vecT, s_ct, s_adasb, s_colps, s_cols, s_bcps, s_bc, s_ht = map(sem, (
            "vec_t", "c_silu", "ada_sb", "col_ps", "cols_ready", "bc_ps", "bc_ready", "ht_ready"))
        s_proj, s_projout = sem("proj_done"), sem("proj_out")
        s_biasr, s_bm, s_z = sem("bias_ready"), sem("bm_ready"), sem("pads_zero")
        s_s, s_sadd, s_nmax, s_p, s_av, s_y = map(sem, ("scores", "scores_biased", "neg_max", "probs", "av", "y_out"))
        s_rope, s_gain = sem("rope_out"), sem("gains_ready")
        s_sg, s_br, s_brout, s_op, s_opout, s_xh2 = map(sem, (
            "sigmoid", "branch", "merged", "outproj", "x2_ready", "xh2_ready"))
        s_log, s_nm2, s_ex, s_aff, s_slot = map(sem, ("logits", "logits_shift", "logits_exp", "aff_ready", "slots_ready"))
        s_dve = sem("dve_chain")
        s_colrow = sem("col_row")
        s_ss, s_rstd, s_nhalf = sem("mean_square"), sem("rstd"), sem("nhalf_ready")
        s_pick, s_gath, s_give, s_xin, s_xt, s_xinT, s_giveT = map(sem, (
            "pick_ready", "gathered", "give_t", "xin_ready", "xin_t", "xin_t_out", "give_t_out"))
        s_silu, s_act, s_at, s_actT, s_ysb, s_cb, s_cbout = map(sem, (
            "silu_done", "act_ready", "act_t", "act_t_out", "y_ready", "combined",
            "added"))
        s_fin, s_out = sem("final"), sem("stored")

        block = ctx.enter_context(nc.Block())

        x_rows = x[0].rearrange("(r j c) d -> r c j d", r=ROWS, j=NT)

        @block.sync
        def _(sp):
            sp.dma_start(vecs[0:8, :], c.rearrange("b (k p) -> (b k) p", p=P)).then_inc(s_vec, 16)
            sp.dma_start(vecs[8:16, :], norm1_g.rearrange("b (k p) -> (b k) p", p=P)).then_inc(s_vec, 16)
            sp.dma_start(vecs[16:24, :], norm2_g.rearrange("b (k p) -> (b k) p", p=P)).then_inc(s_vec, 16)
            sp.dma_start(cst[:, :], consts).then_inc(s_const, 16)
            for r in range(ROWS):
                sp.dma_start(xs[r:P:ROWS, :, :], x_rows[r]).then_inc(s_x, 16)
            sp.dma_start(gains[:, 0, :], q_norm_g.partition_broadcast(P)[:, 0, :]).then_inc(s_small, 16)
            sp.dma_start(gains[:, 1, :], k_norm_g.partition_broadcast(P)[:, 0, :]).then_inc(s_small, 16)
            sp.dma_start(wr[:, :, :], w_router.rearrange("(k p) e -> p k e", p=P)).then_inc(s_small, 16)

            w_in_k = w_in.rearrange("(k p) n -> p k n", p=P)

            def front(m, src, dst):
                if m == 1:
                    sp.wait_ge(s_adaused, 3)
                if m == 12:
                    sp.wait_ge(s_s, 32)
                elif m >= FRONT_SLOTS:
                    sp.wait_ge(s_proj, proj_end(m - FRONT_SLOTS))
                sp.dma_start(dst, src).then_inc(s_w[slot_of(m)], 16)

            k8 = lambda m, n: slot(slot_of(m))[:, 0:KD * n].rearrange("p (k n) -> p k n", k=KD)
            for m in range(3):
                front(m, w_in_k[:, :, 512 * m:512 * m + 512], k8(m, 512))
            front(3, w_in_k[:, :, 2048:2304], k8(3, 256))
            front(4, w_in_k[:, :, 1536:2048], k8(4, 512))
            for g in range(4):
                front(5 + g, w_in_k[:, :, 2304 + 512 * g:2816 + 512 * g], k8(5 + g, 512))
            for m, w in ((9, w_branch_na), (10, w_branch_gqa)):
                front(m, w.rearrange("(k p) n -> p k n", p=P), slot(slot_of(m)).rearrange("p (k n) -> p k n", k=4))
            for h in range(2):
                front(11 + h, w_out.rearrange("(k p) n -> p k n", p=P)[:, :, 512 * h:512 * h + 512], k8(11 + h, 512))

            def expert_tile(e, i):
                if i < 8:
                    g, up, kh = i // 4, i // 2 % 2, i % 2
                    w = (w_exp_up if up else w_exp_gate)[bass.ds(e, 1), 512 * kh:512 * kh + 512, 1024 * g:1024 * g + 1024]
                else:
                    w = w_exp_down[bass.ds(e, 1), 512 * (i - 8):512 * (i - 8) + 512, :]
                sp.dma_start(slot(eslot(i)).rearrange("p (k n) -> p k n", k=4),
                             w.rearrange("a (k p) n -> p (a k) n", p=P)).then_inc(s_w[eslot(i)], 16)

            for i in range(ET):
                if i == 0:
                    sp.wait_ge(s_tdone, B_YG + 4)
                elif i == 2:
                    sp.wait_ge(s_br, 2 * KD)
                elif i == 4:
                    sp.wait_ge(s_op, NT)
                elif i >= RING:
                    sp.wait_ge(s_wused, i - RING + 1)
                expert_tile(0, i)
            with sp.Fori(1, E) as e:
                for i in range(ET):
                    sp.wait_ge(s_wused, e * ET + (i - RING + 1))
                    expert_tile(e, i)
            for j in range(NT):
                sp.wait_ge(s_fin, j + 1)
                for r in range(ROWS):
                    sp.dma_start(out[0].rearrange("(r j c) d -> r c j d", r=ROWS, j=NT)[r][:, j, :],
                                 xs[r:P:ROWS, j, :]).then_inc(s_out, 16)
            sp.wait_ge(s_out, 16 * NT * ROWS)

        @block.gpsimd
        def _(pool):
            nc.gpsimd.memset(ones[:, :], 1.0).then_inc(s_ones, 1)
            nc.gpsimd.memset(nhalf[:, :], -0.5).then_inc(s_nhalf, 1)
            nc.gpsimd.memset(pb[:, :, 0:64], 0.0).then_inc(s_z, 1)
            nc.gpsimd.memset(pb[:, :, 320:384], 0.0).then_inc(s_z, 1)
            for g in range(3):
                pool.dma_start(adab[0:97:32, g, :], b_ada[:, 2048 * g:2048 * g + 2048]
                               .rearrange("a (i n) -> (a i) n", i=4)).then_inc(s_adab, 16)
            n_pow = [0]

            def power(a, n):
                n_pow[0] += 1
                pool.wait_ge(s_ss, n_pow[0])
                nc.gpsimd.tensor_tensor(a, a, nhalf[:, 0:n], ALU.pow).then_inc(s_rstd, 1)

            for m in range(NADA):
                if m == 2:
                    pool.wait_ge(s_nhalf, 1)
                    for j in range(NT):
                        power(stat[:, 8 + j:9 + j], 1)
                if m == 4:
                    pool.wait_ge(s_tdone, B_X + KD)
                    RW = 47
                    for cc in range(16):
                        src = bass.AP(tensor=na_rpb.tensor, offset=15 - cc, ap=[[H * RW, ROWS], [RW, H * ROWS], [1, 32]])
                        pool.dma_start(braw[ROWS * cc:ROWS * cc + ROWS].rearrange("p r h c -> p (r h) c"), src).then_inc(s_rpb, 16)
                if m >= 2:
                    pool.wait_ge(s_adaused, m - 1)
                g, k2 = m // 4, m % 4
                pool.dma_start(ada_slot(m), w_ada[256 * k2:256 * k2 + 256, 2048 * g:2048 * g + 2048]
                               .rearrange("(k p) n -> p k n", p=P)).then_inc(s_ada[m % 2], 16)
            pool.wait_ge(s_biasr, 1)
            pool.wait_ge(s_const, 16)
            for d in range(16):
                j, k0, w, kb, nb, v = NAJ[d // 4]
                h = 2 * (d % 4)
                if d >= 2:
                    pool.wait_ge(s_sadd, d - 1)
                wv = 192 if v else 256
                c0 = 8 if v == 1 else 0
                for i in range(2):
                    last = nc.gpsimd.tensor_tensor(bm[:, d % 2, i, 0:wv],
                                            bias[:, h + i, c0:c0 + wv // 8, :].rearrange("p c r -> p (c r)"),
                                            mask[:, v, 0:wv], ALU.add)
                    last.then_inc(s_bm, 1)
                if v == 1:
                    nc.gpsimd.tensor_copy(bm[:, d % 2, :, 192:256],
                                          mask[:, 1, 192:256].unsqueeze(1).broadcast_to([P, 2, 64])).then_inc(s_bm, 1)
                if d % 2 and d >= 3:
                    power(stat[:, 16:18] if d <= 9 else stat[:, 16:24], 2 if d <= 9 else 8)
            power(stat[:, 16:24], 8)
            pool.wait_ge(s_sadd, 16)
            pool.wait_ge(s_y, 16)
            pool.dma_start(fing, final_g.rearrange("(a n) -> a n", a=1).partition_broadcast(P)[:, 0, :]).then_inc(s_fing, 16)
            for j in range(2 * NT):
                power(stat[:, 8 + j % NT:9 + j % NT], 1)

        bm_count = lambda d: 2 * (d + 1) + max(0, d - 11)

        @block.scalar
        def _(act_):
            act_.wait_ge(s_vecT, 1)
            nc.scalar.activation(cT, ps[:, 7, 0:8], ACT.Silu).then_inc(s_ct, 1)

            copy = lambda o, i: nc.scalar.activation(o, i, ACT.Copy)
            for k in range(1, KD, 2):
                act_.wait_ge(s_tdone, B_X + k + 1)
                copy(ht[:, k, :], ps[:, 4 + (B_X + k) % 2, :]).then_inc(s_tout[1], 1)
            act_.wait_ge(s_cols, 1)
            act_.wait_ge(s_tout[0], KD // 2)
            act_.wait_ge(s_tout[1], KD // 2)
            for k in range(KD):
                nc.scalar.activation(ht[:, k, :], ht[:, k, :], ACT.Identity, bias=s1[:, k:k + 1],
                                     scale=a1[:, k:k + 1]).then_inc(s_ht, 1)

            def proj_out(n):
                act_.wait_ge(s_proj, n + 1)
                src = ps[:, proj_bank(n), :]
                if n < G_K:
                    o = nc.scalar.activation(qk[:, n, :], src, ACT.Copy, scale=QS)
                elif n < G_V:
                    o = copy(qk[:, n, :], src)
                elif n < G_KV:
                    if n == G_V:
                        act_.wait_ge(s_colps, 2)
                    o = copy(vy[:, n - G_V, :], src)
                elif n < G_QG:
                    o = copy(kvg[:, n - G_KV, :], src[:, 0:256])
                elif n < G_GATE:
                    if n == G_QG:
                        act_.wait_ge(s_biasr, 1)
                    o = copy(qy[:, 0, n - G_QG, :].rearrange("p (i g d) -> p g i d", g=2, i=4),
                             src.rearrange("p (g i d) -> p g i d", g=2, i=4))
                else:
                    o = copy(sig[:, n - G_GATE, :], src)
                o.then_inc(s_projout, 1)

            def exps(d):
                for i in range(2):
                    u = 2 * d + i
                    act_.wait_ge(s_nmax, d + 1)
                    if u >= 4:
                        act_.wait_ge(s_tdone, (B_NA if d < 18 else B_GQ) + (u - 4 if d < 18 else u - 36) + 1)
                    else:
                        act_.wait_ge(s_z, 2)
                    if d < 16:
                        j, k0, w, kb, nb, v = NAJ[d // 4]
                        o, s = pb[:, u % 4, k0 - kb:k0 - kb + w], ssb[:, i, 0:w]
                    else:
                        o, s = pb[:, u % 4, :], ps[:, 2 * (d % 2) + i, :]
                    nc.scalar.activation(o, s, ACT.Exp, bias=nmax[:, u:u + 1],
                                         accum_out=rsum[:, u:u + 1]).then_inc(s_p, 1)

            def pt_out(d):
                base = B_NA if d < 16 else B_GQ - 32
                for i in range(2):
                    n = base + 2 * d + i
                    if n % 2:
                        act_.wait_ge(s_tdone, n + 1)
                        if d:
                            act_.wait_ge(s_av, d)
                        w = P * NAJ[d // 4][4] if d < 16 else T
                        copy(ptb[:, i, 0:w], ps[:, 4 + n % 2, 0:w]).then_inc(s_tout[1], 1)

            for n in range(G_KV):
                proj_out(n)
            for d in range(17):
                if d < 16:
                    exps(d)
                    if d % 2:
                        proj_out(G_KV + d // 2)
                if d:
                    pt_out(d - 1)
            proj_out(G_GATE)
            for i in range(4):
                n = B_YN + i
                if n % 2:
                    act_.wait_ge(s_tdone, n + 1)
                    copy(ytn[:, i, :], ps[:, 4 + n % 2, :]).then_inc(s_tout[1], 1)
            if B_K % 2:
                act_.wait_ge(s_tdone, B_K + 1)
                copy(kt, ps[:, 4 + B_K % 2, :]).then_inc(s_tout[1], 1)
            for j in range(NT):
                n = B_Q + j
                if n % 2:
                    act_.wait_ge(s_tdone, n + 1)
                    copy(qt[:, :, P * j:P * j + P], ps[:, 4 + n % 2, :].rearrange("p (b t) -> p b t", b=4)).then_inc(s_tout[1], 1)
            for d in range(16, 33):
                if d < 32:
                    exps(d)
                if d > 16:
                    pt_out(d - 1)
                if d < 31:
                    proj_out(G_GATE + 1 + d - 16)
            for i in range(4):
                n = B_YG + i
                if n % 2:
                    act_.wait_ge(s_tdone, n + 1)
                    copy(ytg[:, i, :], ps[:, 4 + n % 2, :]).then_inc(s_tout[1], 1)
            act_.wait_ge(s_projout, N_PROJ)
            for b in range(KD):
                for br in range(2):
                    nc.scalar.activation(sig[:, KD * br + b, :], sig[:, KD * br + b, :], ACT.Sigmoid).then_inc(s_sg, 1)
            for k in range(KD):
                n = B_X2 + k
                if n % 2:
                    act_.wait_ge(s_tdone, n + 1)
                    nc.scalar.activation(h2t[:, k, :], ps[:, 4 + n % 2, :], ACT.Identity, bias=s2[:, k:k + 1],
                                         scale=a2[:, k:k + 1]).then_inc(s_tout[1], 1)
            act_.wait_ge(s_nm2, 1)
            nc.scalar.activation(aff[:, :, :], aff[:, :, :], ACT.Exp).then_inc(s_ex, 1)
            if B_AFF % 2:
                act_.wait_ge(s_tdone, B_AFF + 1)
                copy(work.rearrange("e (r c) -> e r c", c=COLS),
                     ps[0:E, 4 + B_AFF % 2, :].rearrange("e (c r) -> e r c", r=ROWS)).then_inc(s_tout[1], 1)
            if B_SLOT % 2:
                act_.wait_ge(s_tdone, B_SLOT + 1)
                copy(slots[:, :, 0:E], ps[:, 4 + B_SLOT % 2, 0:NT * E].rearrange("p (j e) -> p j e", j=NT)).then_inc(s_tout[1], 1)

            with act_.Fori(0, E) as e:
                act_.wait_ge(s_xt, e + 1)
                for k in range(KD):
                    c0 = P * (k % 4) + CAP * (k // 4)
                    nc.scalar.activation(xinT[:, k, :], ps[:, 5, c0:c0 + CAP], ACT.Identity, bias=s2[:, k:k + 1],
                                         scale=a2[:, k:k + 1]).then_inc(s_xinT, 1)
                for g in range(2):
                    act_.wait_ge(s_wused, e * ET + (4 * g + 2))
                    nc.scalar.activation(silu[:, g, :], ps[:, 2 * g, :], ACT.Silu).then_inc(s_silu, 1)

        @block.vector
        def _(dve):
            chain = [0]

            def link(ins):
                chain[0] += 1
                ins.then_inc(s_dve, 1)
                dve.wait_ge(s_dve, chain[0])

            n_pow = [0]

            def mean_square(j, scratch):
                link(nc.vector.tensor_tensor_reduce(out=scratch[:, j, :], in0=xs[:, j, :], in1=xs[:, j, :], scale=1.0 / D,
                                                    scalar=0.0, op0=ALU.mult, op1=ALU.add, accum_out=stat[:, j:j + 1]))
                nc.vector.tensor_scalar(stat[:, 8 + j:9 + j], stat[:, j:j + 1], EPS, None, ALU.add).then_inc(s_ss, 1)

            def rstd_in():
                n_pow[0] += 1
                dve.wait_ge(s_rstd, n_pow[0])

            def normalise(j, dst, ready):
                rstd_in()
                nc.vector.tensor_scalar(dst[:, j, :], xs[:, j, :], stat[:, 8 + j:9 + j], None, ALU.mult).then_inc(ready, 1)

            dve.wait_ge(s_x, 16 * ROWS)
            for j in range(NT):
                mean_square(j, xh)
            for j in range(NT):
                normalise(j, xh, s_xh)
            dve.wait_ge(s_ct, 1)
            link(nc.vector.tensor_copy(col[:, 1:3, :], ps[:, 7, 8:24].rearrange("p (v k) -> p v k", v=2)))
            for k in range(0, KD, 2):
                dve.wait_ge(s_tdone, B_X + k + 1)
                nc.vector.tensor_copy(ht[:, k, :], ps[:, 4, :]).then_inc(s_tout[0], 1)

            def ada_rows(g):
                dve.wait_ge(s_adaused, 4 * (g + 1))
                dve.wait_ge(s_adab, 48)
                for i in range(4):
                    q = 32 * i
                    gate = (g == 1 and i < 2) or (g == 2 and i >= 2)
                    dst = grow[q:q + 1, :] if gate else adar[q:q + 1, min(g, 1), :]
                    nc.vector.tensor_tensor(dst, ps[q:q + 1, 6, :], adab[q:q + 1, g, :], ALU.add).then_inc(s_adasb, 1)

            ada_rows(0)
            dve.wait_ge(s_colps, 1)
            link(nc.vector.tensor_copy(s1, ps[:, 2, 0:8]))
            nc.vector.scalar_tensor_tensor(out=a1, in0=ps[:, 2, 8:16], scalar=1.0, in1=n1c, op0=ALU.add,
                                           op1=ALU.mult).then_inc(s_cols, 1)
            dve.wait_ge(s_rpb, 16 * 16)
            nc.vector.tensor_copy(bias[:, :, :, :].rearrange("p h c r -> p r h c"), braw[:, ::-1, :, :]).then_inc(s_biasr, 1)
            dve.wait_ge(s_small, 48)
            nc.vector.tensor_scalar(gains[:, 1, :], gains[:, 1, :], HD ** 0.5, None, ALU.mult).then_inc(s_gain, 1)
            ada_rows(1)
            ada_rows(2)
            dve.wait_ge(s_colps, 2)
            link(nc.vector.tensor_copy(s2, ps[:, 2, 16:24]))
            nc.vector.scalar_tensor_tensor(out=a2, in0=ps[:, 2, 24:32], scalar=1.0, in1=n2c, op0=ALU.add,
                                           op1=ALU.mult).then_inc(s_cols, 1)

            def rope(src, dst, nh, gain, j):
                w = nh * HD
                tmp = rt[:, 0:w].rearrange("p (h d) -> p h d", h=nh)
                t2 = rt[:, 512:512 + w // 2].rearrange("p (h d) -> p h d", h=nh)
                t3 = rt[:, 768:768 + w // 2].rearrange("p (h d) -> p h d", h=nh)
                st = stat[:, 16:16 + nh]
                link(nc.vector.tensor_tensor(tmp, src, src, ALU.mult))
                link(nc.vector.tensor_reduce(out=st, in_=tmp, axis=X, op=ALU.add))
                nc.vector.tensor_scalar(st, st, HD * EPS, None, ALU.add).then_inc(s_ss, 1)
                rstd_in()
                link(nc.vector.tensor_tensor(tmp, src, st.unsqueeze(2).broadcast_to([P, nh, HD]), ALU.mult))
                link(nc.vector.tensor_tensor(tmp, tmp, gain.unsqueeze(1).broadcast_to([P, nh, HD]), ALU.mult))
                even, odd = tmp[:, :, 0:HD:2], tmp[:, :, 1:HD:2]
                cj = cos[:, j, :].unsqueeze(1).broadcast_to([P, nh, HD // 2])
                sj = sin[:, j, :].unsqueeze(1).broadcast_to([P, nh, HD // 2])
                nc.vector.tensor_tensor(t2, even, cj, ALU.mult)
                link(nc.vector.tensor_tensor(t3, odd, sj, ALU.mult))
                link(nc.vector.tensor_tensor(dst[:, :, 0:HD:2], t2, t3, ALU.subtract))
                nc.vector.tensor_tensor(t2, even, sj, ALU.mult)
                link(nc.vector.tensor_tensor(t3, odd, cj, ALU.mult))
                nc.vector.tensor_tensor(dst[:, :, 1:HD:2], t2, t3, ALU.add).then_inc(s_rope, 1)

            def softmax(d):
                if d < 16:
                    j, k0, w, kb, nb, v = NAJ[d // 4]
                    dve.wait_ge(s_s, 2 * d + 2)
                    dve.wait_ge(s_bm, bm_count(d))
                    if d:
                        dve.wait_ge(s_p, 2 * d)
                    nc.vector.tensor_tensor(ssb[:, :, 0:w], ps[:, 2 * (d % 2):2 * (d % 2) + 2, 0:w],
                                            bm[:, d % 2, :, 0:w], ALU.add).then_inc(s_sadd, 1)
                    dve.wait_ge(s_sadd, d + 1)
                    src = ssb[:, :, 0:w]
                else:
                    dve.wait_ge(s_s, 2 * d + 2)
                    src = ps[:, 2 * (d % 2):2 * (d % 2) + 2, :]
                nc.vector.tensor_reduce(out=nmax[:, 2 * d:2 * d + 2], in_=src, axis=X, op=ALU.max,
                                        negate=True).then_inc(s_nmax, 1)

            def pt_out(d):
                base = B_NA if d < 16 else B_GQ - 32
                for i in range(2):
                    n = base + 2 * d + i
                    if n % 2 == 0:
                        dve.wait_ge(s_tdone, n + 1)
                        if d:
                            dve.wait_ge(s_av, d)
                        w = P * NAJ[d // 4][4] if d < 16 else T
                        nc.vector.tensor_copy(ptb[:, i, 0:w], ps[:, 4, 0:w]).then_inc(s_tout[0], 1)

            def y_out(d):
                dve.wait_ge(s_p, 2 * d + 2)
                link(nc.vector.reciprocal(rinv[:, 2 * d:2 * d + 2], rsum[:, 2 * d:2 * d + 2]))
                dve.wait_ge(s_av, d + 1)
                if d < 16:
                    j, h, step = NAJ[d // 4][0], 2 * (d % 4), 1
                else:
                    j, h, step = (d - 16) // 4, d % 4, 4
                    if d == 16:
                        dve.wait_ge(s_tdone, B_YN + 4)
                dst = ytok[:, j, :].rearrange("p (h d) -> p h d", h=H)[:, h:h + step + 1:step, :]
                nc.vector.tensor_tensor(dst, ps[:, 6, 0:P].rearrange("p (h d) -> p h d", h=2),
                                        rinv[:, 2 * d:2 * d + 2].unsqueeze(2).broadcast_to([P, 2, HD]),
                                        ALU.mult).then_inc(s_y, 1)

            dve.wait_ge(s_gain, 1)
            for d in range(18):
                if d < 16:
                    softmax(d)
                if 1 <= d <= 16:
                    pt_out(d - 1)
                if d >= 2:
                    y_out(d - 2)
                if d % 2 and 3 <= d <= 9:
                    j = (d - 3) // 2
                    dve.wait_ge(s_projout, G_KV + j + 1)
                    kk = kvg[:, j, 0:P].rearrange("p (h d) -> p h d", h=2)
                    rope(kk, kk, 2, gains[:, 1, :], j)
                if d % 2 and d >= 11:
                    j = (d - 11) // 2
                    dve.wait_ge(s_projout, G_QG + j + 1)
                    qq = qy[:, 0, j, :].rearrange("p (h d) -> p h d", h=H)
                    rope(qq, qq, H, gains[:, 0, :], j)
            for i in range(4):
                n = B_YN + i
                if n % 2 == 0:
                    dve.wait_ge(s_tdone, n + 1)
                    nc.vector.tensor_copy(ytn[:, i, :], ps[:, 4, :]).then_inc(s_tout[0], 1)
            if B_K % 2 == 0:
                dve.wait_ge(s_tdone, B_K + 1)
                nc.vector.tensor_copy(kt, ps[:, 4, :]).then_inc(s_tout[0], 1)
            for j in range(NT):
                n = B_Q + j
                if n % 2 == 0:
                    dve.wait_ge(s_tdone, n + 1)
                    nc.vector.tensor_copy(qt[:, :, P * j:P * j + P],
                                          ps[:, 4, :].rearrange("p (b t) -> p b t", b=4)).then_inc(s_tout[0], 1)
            for d in range(16, 34):
                if d < 32:
                    softmax(d)
                if 17 <= d <= 32:
                    pt_out(d - 1)
                if d >= 18:
                    y_out(d - 2)
            for i in range(4):
                n = B_YG + i
                if n % 2 == 0:
                    dve.wait_ge(s_tdone, n + 1)
                    nc.vector.tensor_copy(ytg[:, i, :], ps[:, 4, :]).then_inc(s_tout[0], 1)
            dve.wait_ge(s_bcps, 1)
            dve.wait_ge(s_bm, bm_count(15))
            nc.vector.tensor_copy(gate1, ps[:, 2:4, :].rearrange("p a n -> p (a n)")).then_inc(s_bc, 1)
            nc.vector.tensor_copy(gate2, ps[:, 7, :]).then_inc(s_bc, 1)

            for b in range(KD):
                q = 2 * (b % 2)
                dve.wait_ge(s_sg, 2 * b + 2)
                dve.wait_ge(s_br, 2 * b + 2)
                link(nc.vector.tensor_tensor(ht[:, b, :], sig[:, b, :], ps[:, q, :], ALU.mult))
                link(nc.vector.tensor_tensor(sig[:, KD + b, :], sig[:, KD + b, :], ps[:, q + 1, :], ALU.mult))
                nc.vector.tensor_tensor(ht[:, b, :], ht[:, b, :], sig[:, KD + b, :], ALU.add).then_inc(s_brout, 1)
            dve.wait_ge(s_brout, KD)
            for j in range(NT):
                q = 2 * (j % 2)
                dve.wait_ge(s_op, j + 1)
                tmp = xh2[:, j, :]
                link(nc.vector.tensor_tensor(tmp, ps[:, q:q + 2, :].rearrange("p a n -> p (a n)"), gate1, ALU.mult))
                nc.vector.tensor_tensor(xs[:, j, :], xs[:, j, :], tmp, ALU.add).then_inc(s_opout, 1)
                dve.wait_ge(s_opout, j + 1)
                mean_square(j, xh2)
                if j:
                    normalise(j - 1, xh2, s_xh2)
            normalise(NT - 1, xh2, s_xh2)
            for k in range(KD):
                n = B_X2 + k
                if n % 2 == 0:
                    dve.wait_ge(s_tdone, n + 1)
                    nc.vector.tensor_scalar(h2t[:, k, :], ps[:, 4, :], a2[:, k:k + 1], s2[:, k:k + 1], ALU.mult,
                                            ALU.add).then_inc(s_tout[0], 1)
            dve.wait_ge(s_log, 1)
            lg = ps[:, 7, 0:NT * E].rearrange("p (j e) -> p j e", j=NT)
            bce = lambda a: a.unsqueeze(2).broadcast_to([P, NT, E])
            link(nc.vector.tensor_reduce(out=stat[:, 48:52], in_=lg, axis=X, op=ALU.max))
            nc.vector.tensor_tensor(aff[:, :, :], lg, bce(stat[:, 48:52]), ALU.subtract).then_inc(s_nm2, 1)
            dve.wait_ge(s_ex, 1)
            link(nc.vector.tensor_reduce(out=stat[:, 52:56], in_=aff[:, :, :], axis=X, op=ALU.add))
            link(nc.vector.reciprocal(stat[:, 56:60], stat[:, 52:56]))
            nc.vector.tensor_tensor(aff[:, :, :], aff[:, :, :], bce(stat[:, 56:60]), ALU.mult).then_inc(s_aff, 1)
            nc.vector.memset(onesr, 1.0)
            nc.vector.memset(slots[:, :, E:E + 1], 0.0).then_inc(s_cbout, 1)
            if B_AFF % 2 == 0:
                dve.wait_ge(s_tdone, B_AFF + 1)
                link(nc.vector.tensor_copy(work.rearrange("e (r c) -> e r c", c=COLS),
                                           ps[0:E, 4, :].rearrange("e (c r) -> e r c", r=ROWS)))
            else:
                dve.wait_ge(s_tout[1], B_AFF // 2 + 1)
            for r in range(CAP // 8):
                link(nc.vector.max(out=top8[:, 8 * r:8 * r + 8], in_=work))
                link(nc.vector.match_replace(out=work, in_to_replace=top8[:, 8 * r:8 * r + 8], in_values=work,
                                             imm_value=-1.0))
            link(nc.vector.tensor_scalar(sel, work, 0.0, None, ALU.is_lt))
            link(nc.vector.tensor_tensor_scan(out=cum, data0=onesr, data1=sel, initial=0.0, op0=ALU.mult, op1=ALU.add))
            nc.vector.tensor_tensor(slot_e.rearrange("e (c r) -> e r c", r=ROWS), cum.rearrange("e (r c) -> e r c", c=COLS),
                                    sel.rearrange("e (r c) -> e r c", c=COLS), ALU.mult).then_inc(s_slot, 1)
            if B_SLOT % 2 == 0:
                dve.wait_ge(s_tdone, B_SLOT + 1)
                nc.vector.tensor_copy(slots[:, :, 0:E], ps[:, 4, 0:NT * E].rearrange("p (j e) -> p j e", j=NT)).then_inc(s_tout[0], 1)
                dve.wait_ge(s_tout[0], B_SLOT // 2 + 1)
            else:
                dve.wait_ge(s_tout[1], B_SLOT // 2 + 1)

            def one_hots(e, waits=True):
                for j in range(NT):
                    sc, af = slots[:, j, bass.ds(e, 1)], aff[:, j, bass.ds(e, 1)]
                    nc.vector.tensor_scalar(pick[:, j, :], iota[:, 0:CAP], sc, None, ALU.is_equal)
                    last = nc.vector.tensor_scalar(give[:, j, :], iota, sc, af, ALU.is_equal, ALU.mult)
                last.then_inc(s_pick, 1)

            one_hots(0)

            def expert(e, more):
                dve.wait_ge(s_gath, e + 1)
                nc.vector.tensor_copy(xin, ps[:, 7, :]).then_inc(s_xin, 1)
                dve.wait_ge(s_give, e + 1)
                nc.vector.tensor_copy(giveT, ps[:, 6, :]).then_inc(s_giveT, 1)
                if more:
                    one_hots(e + 1)
                for g in range(2):
                    dve.wait_ge(s_silu, 2 * e + g + 1)
                    dve.wait_ge(s_wused, e * ET + (4 * g + 4))
                    nc.vector.tensor_tensor(act[:, g, :], silu[:, g, :], ps[:, 2 * g + 1, :], ALU.mult).then_inc(s_act, 1)
                for g in range(2):
                    dve.wait_ge(s_at, 2 * e + g + 1)
                    dst = actT[:, 8 * g:8 * g + 8, :].rearrange("p (h b) s -> p b h s", h=2)
                    nc.vector.tensor_copy(dst, ps[:, 5 + g, :].rearrange("p (b h s) -> p b h s", b=4, h=2)).then_inc(s_actT, 1)
                dve.wait_ge(s_wused, e * ET + ET)
                nc.vector.tensor_tensor(ysb, ps[:, 4, :], gate2, ALU.mult).then_inc(s_ysb, 1)
                for j in range(NT):
                    q = 2 * (j % 2)
                    dve.wait_ge(s_cb, 4 * e + j + 1)
                    nc.vector.tensor_tensor(xs[:, j, :], xs[:, j, :], ps[:, q:q + 2, :].rearrange("p a n -> p (a n)"),
                                            ALU.add).then_inc(s_cbout, 1)

            with dve.Fori(0, E - 1) as e:
                expert(e, True)
            expert(E - 1, False)
            dve.wait_ge(s_cbout, NT * E + 1)
            dve.wait_ge(s_fing, 16)
            def final(j):
                rstd_in()
                nc.vector.scalar_tensor_tensor(out=xs[:, j, :], in0=xs[:, j, :], scalar=stat[:, 8 + j:9 + j], in1=fing,
                                               op0=ALU.mult, op1=ALU.mult).then_inc(s_fin, 1)

            for j in range(NT):
                mean_square(j, xh2)
                if j:
                    final(j - 1)
            final(NT - 1)

        @block.tensor
        def _(pe):
            mm = nc.tensor.matmul
            pe.wait_ge(s_vec, 48)
            pe.wait_ge(s_const, 16)
            nc.tensor.transpose(ps[:, 7, 0:24], vecs[:, :], ident[0:24, 0:24]).then_inc(s_vecT, 1)

            def bank_free(n):
                if n >= 2:
                    pe.wait_ge(s_tout[n % 2], n // 2)

            def batches_out(n):
                pe.wait_ge(s_tout[0], (n + 1) // 2)
                pe.wait_ge(s_tout[1], n // 2)

            pe.wait_ge(s_xh, NT)
            for k in range(KD):
                n = B_X + k
                bank_free(n)
                for j in range(NT):
                    last = nc.tensor.transpose(ps[:, 4 + n % 2, P * j:P * j + P], xh[:, j, P * k:P * k + P], ident)
                last.then_inc(s_tdone, 1)

            pe.wait_ge(s_ct, 1)
            pe.wait_ge(s_ones, 1)

            def ada(m):
                g, k2 = m // 4, m % 4
                pe.wait_ge(s_ada[m % 2], 16 * (m // 2 + 1))
                if g and k2 == 0:
                    pe.wait_ge(s_adasb, 4 * g)
                for kk in range(2):
                    k = 2 * k2 + kk
                    for i in range(4):
                        last = mm(ps[32 * i:32 * i + 1, 6, :], cT[:, k:k + 1], ada_slot(m)[:, kk, 512 * i:512 * i + 512],
                                  start=(k == 0), stop=(k == KD - 1), skip_group_check=True)
                last.then_inc(s_adaused, 1)

            n_cols = [0]

            def columns(g, row0, col0):
                for b in range(KD):
                    if b % 4 == 0 and n_cols[0]:
                        pe.wait_ge(s_colrow, n_cols[0])
                    q = 32 * (row0 + b // 4)
                    last = mm(ps[:, 2, col0 + b:col0 + b + 1], adar[q:q + 1, g, P * (b % 4):P * (b % 4) + P],
                              ones[q:q + 1, 0:1], start=True, stop=True)
                    if b == 3:
                        last.then_inc(s_colrow, 1)
                        n_cols[0] += 1
                return last

            for m in range(4):
                ada(m)
            pe.wait_ge(s_adasb, 4)
            columns(0, 0, 0).then_inc(s_colrow, 1)
            n_cols[0] += 1
            columns(0, 2, 8).then_inc(s_colps, 1)

            def proj(n, k0=0, k1=KD):
                m = proj_tile(n)
                width = 256 if m == 3 else 512
                w = slot(slot_of(m))[:, 0:KD * width].rearrange("p (k n) -> p k n", k=KD)
                if k0 == 0:
                    pe.wait_ge(s_w[slot_of(m)], 16 * uses_of(m))
                    if n >= G_KV:
                        pe.wait_ge(s_projout, n)
                    elif n >= 4:
                        pe.wait_ge(s_projout, n - 3)
                for k in range(k0, k1):
                    if n == 0:
                        pe.wait_ge(s_ht, k + 1)
                    if n < G_V or n >= G_GATE:
                        b = n % 4
                        last = mm(ps[:, proj_bank(n), :], w[:, k, P * b:P * b + P], ht[:, k, :], start=(k == 0),
                                  stop=(k == KD - 1))
                    else:
                        j = n % 4
                        last = mm(ps[:, proj_bank(n), 0:width], ht[:, k, P * j:P * j + P], w[:, k, :], start=(k == 0),
                                  stop=(k == KD - 1))
                if k1 == KD:
                    last.then_inc(s_proj, 1)

            for n in range(8):
                proj(n)
                ada(4 + n)
            pe.wait_ge(s_adasb, 12)
            pe.wait_ge(s_cols, 1)
            columns(1, 2, 16).then_inc(s_colrow, 1)
            n_cols[0] += 1
            columns(1, 0, 24).then_inc(s_colps, 1)
            for n in range(8, G_KV):
                proj(n)

            def scores(d):
                if d >= 18:
                    pe.wait_ge(s_p, 2 * d - 2)
                elif d >= 2:
                    pe.wait_ge(s_sadd, d - 1)
                for i in range(2):
                    r = slice(HD * i, HD * i + HD)
                    if d < 16:
                        j, k0, w, kb, nb, v = NAJ[d // 4]
                        q, k = qk[r, d % 4, P * j:P * j + P], qk[r, 4 + d % 4, k0:k0 + w]
                    else:
                        j, w = (d - 16) // 4, T
                        q, k = qt[r, d % 4, P * j:P * j + P], kt[r, :]
                    mm(ps[:, 2 * (d % 2) + i, 0:w], q, k, start=True, stop=True).then_inc(s_s, 1)

            def transposes(d):
                base = B_NA if d < 16 else B_GQ - 32
                for i in range(2):
                    u = 2 * d + i
                    n = base + u
                    pe.wait_ge(s_p, u + 1)
                    bank_free(n)
                    nb = NAJ[d // 4][4] if d < 16 else NT
                    for b in range(nb):
                        last = nc.tensor.transpose(ps[:, 4 + n % 2, P * b:P * b + P], pb[:, u % 4, P * b:P * b + P], ident)
                    last.then_inc(s_tdone, 1)

            def weighted(d):
                base = B_NA if d < 16 else B_GQ - 32
                batches_out(base + 2 * d + 2)
                if d:
                    pe.wait_ge(s_y, d)
                for i in range(2):
                    nb = NAJ[d // 4][4] if d < 16 else NT
                    for b in range(nb):
                        if d < 16:
                            v = vy[:, NAJ[d // 4][3] // P + b, HD * (2 * (d % 4) + i):HD * (2 * (d % 4) + i) + HD]
                        else:
                            v = kvg[:, b, P + HD * i:P + HD * i + HD]
                        last = mm(ps[:, 6, HD * i:HD * i + HD], ptb[:, i, P * b:P * b + P], v, start=(b == 0),
                                  stop=(b == nb - 1))
                last.then_inc(s_av, 1)

            pe.wait_ge(s_projout, G_KV)
            pe.wait_ge(s_cols, 2)
            for d in range(18):
                if d < 16:
                    scores(d)
                if d >= 2:
                    weighted(d - 2)
                if d < 16:
                    proj(G_KV + d // 2, 4 * (d % 2), 4 * (d % 2) + 4)
                if 1 <= d <= 16:
                    transposes(d - 1)
            proj(G_GATE)
            pe.wait_ge(s_y, 16)
            for i in range(4):
                n = B_YN + i
                bank_free(n)
                for j in range(NT):
                    last = nc.tensor.transpose(ps[:, 4 + n % 2, P * j:P * j + P], ytok[:, j, P * i:P * i + P], ident)
                last.then_inc(s_tdone, 1)
            pe.wait_ge(s_rope, 8)
            bank_free(B_K)
            for j in range(NT):
                last = nc.tensor.transpose(ps[:, 4 + B_K % 2, P * j:P * j + P], kvg[:, j, 0:P], ident)
            last.then_inc(s_tdone, 1)
            for j in range(NT):
                n = B_Q + j
                bank_free(n)
                for b in range(4):
                    last = nc.tensor.transpose(ps[:, 4 + n % 2, P * b:P * b + P], qy[:, 0, j, P * b:P * b + P], ident)
                last.then_inc(s_tdone, 1)
            batches_out(B_GQ)
            for d in range(16, 34):
                if d < 32:
                    scores(d)
                if d >= 18:
                    weighted(d - 2)
                if d < 31:
                    proj(G_GATE + 1 + d - 16)
                if 17 <= d <= 32:
                    transposes(d - 1)
            pe.wait_ge(s_y, 32)
            for i in range(4):
                n = B_YG + i
                bank_free(n)
                for j in range(NT):
                    last = nc.tensor.transpose(ps[:, 4 + n % 2, P * j:P * j + P], ytok[:, j, P * i:P * i + P], ident)
                last.then_inc(s_tdone, 1)
            pe.wait_ge(s_projout, N_PROJ)
            pe.wait_ge(s_p, 64)
            for i in range(2):
                mm(ps[:, 2 + i, :], ones[32 * i:32 * i + 1, :], grow[32 * i:32 * i + 1, :], start=True, stop=True)
            for h in range(2):
                q = 64 + 32 * h
                last = mm(ps[64 * h:64 * h + 64, 7, :], ones[q:q + 1, 0:64], grow[q:q + 1, :], start=True, stop=True)
            last.then_inc(s_bcps, 1)

            batches_out(B_YG + 4)
            for b in range(KD):
                if b == 1:
                    pe.wait_ge(s_bc, 2)
                if b >= 2:
                    pe.wait_ge(s_brout, b - 1)
                for br, y in ((0, ytn), (1, ytg)):
                    m = 9 + br
                    if b == 0:
                        pe.wait_ge(s_w[slot_of(m)], 16 * uses_of(m))
                    w = slot(slot_of(m)).rearrange("p (k n) -> p k n", k=4)
                    for k in range(4):
                        last = mm(ps[:, 2 * (b % 2) + br, :], w[:, k, P * b:P * b + P], y[:, k, :], start=(k == 0),
                                  stop=(k == 3))
                    last.then_inc(s_br, 1)
            pe.wait_ge(s_brout, KD)
            for h in range(2):
                pe.wait_ge(s_w[slot_of(11 + h)], 16 * uses_of(11 + h))
            for j in range(NT):
                if j >= 2:
                    pe.wait_ge(s_opout, j - 1)
                for h in range(2):
                    w = slot(slot_of(11 + h)).rearrange("p (k n) -> p k n", k=KD)
                    for k in range(KD):
                        last = mm(ps[:, 2 * (j % 2) + h, :], ht[:, k, P * j:P * j + P], w[:, k, :], start=(k == 0),
                                  stop=(k == KD - 1))
                last.then_inc(s_op, 1)

            pe.wait_ge(s_xh2, NT)
            for k in range(KD):
                n = B_X2 + k
                bank_free(n)
                for j in range(NT):
                    last = nc.tensor.transpose(ps[:, 4 + n % 2, P * j:P * j + P], xh2[:, j, P * k:P * k + P], ident)
                last.then_inc(s_tdone, 1)
            batches_out(B_X2 + KD)
            for j in range(NT):
                for k in range(KD):
                    last = mm(ps[:, 7, E * j:E * j + E], h2t[:, k, P * j:P * j + P], wr[:, k, :], start=(k == 0),
                              stop=(k == KD - 1))
            last.then_inc(s_log, 1)
            pe.wait_ge(s_aff, 1)
            bank_free(B_AFF)
            for j in range(NT):
                last = nc.tensor.transpose(ps[0:E, 4 + B_AFF % 2, P * j:P * j + P], aff[:, j, :], ident)
            last.then_inc(s_tdone, 1)
            pe.wait_ge(s_slot, 1)
            bank_free(B_SLOT)
            for j in range(NT):
                last = nc.tensor.transpose(ps[:, 4 + B_SLOT % 2, E * j:E * j + E], slot_e[:, P * j:P * j + P],
                                           ident[0:E, 0:E])
            last.then_inc(s_tdone, 1)

            def tile_in(e, i):
                s = eslot(i)
                pe.wait_ge(s_w[s], e * (16 * ET // RING) + 16 * (FRONT_USES[s] + i // RING + 1))
                return slot(s).rearrange("p (k n) -> p k n", k=4)

            with pe.Fori(0, E) as e:
                pe.wait_ge(s_pick, e + 1)
                for j in range(NT):
                    for h in range(2):
                        last = mm(ps[64 * h:64 * h + 64, 7, :], pick[:, j, :], xh2[:, j, 512 * h:512 * h + 512],
                                  start=(j == 0), stop=(j == NT - 1), skip_group_check=True)
                last.then_inc(s_gath, 1)
                for j in range(NT):
                    last = nc.tensor.transpose(ps[:, 6, P * j:P * j + P], give[:, j, :], ident)
                last.then_inc(s_give, 1)
                pe.wait_ge(s_xin, e + 1)
                for b in range(4):
                    last = nc.tensor.transpose(ps[:, 5, P * b:P * b + P], xin[:, P * b:P * b + P], ident)
                last.then_inc(s_xt, 1)
                pe.wait_ge(s_xinT, (e + 1) * KD)
                pe.wait_ge(s_cbout, e * NT + 1)
                for g in range(2):
                    for up in range(2):
                        for kh in range(2):
                            w = tile_in(e, 4 * g + 2 * up + kh)
                            for kk in range(4):
                                for h in range(2):
                                    last = mm(ps[64 * h:64 * h + 64, 2 * g + up, :], xinT[:, 4 * kh + kk, :],
                                              w[:, kk, 512 * h:512 * h + 512], start=(kh + kk == 0),
                                              stop=(kh + kk == 4), skip_group_check=True)
                            last.then_inc(s_wused, 1)
                for g in range(2):
                    pe.wait_ge(s_act, 2 * e + (g + 1))
                    if g:
                        pe.wait_ge(s_giveT, e + 1)
                    for b in range(4):
                        last = nc.tensor.transpose(ps[:, 5 + g, P * b:P * b + P], act[:, g, P * b:P * b + P], ident)
                    last.then_inc(s_at, 1)
                for i in range(8, 12):
                    if i % 2 == 0:
                        pe.wait_ge(s_actT, 2 * e + (i // 2 - 3))
                    w = tile_in(e, i)
                    for kk in range(4):
                        f = 4 * (i - 8) + kk
                        for h in range(2):
                            last = mm(ps[64 * h:64 * h + 64, 4, :], actT[:, f, :], w[:, kk, 512 * h:512 * h + 512],
                                      start=(f == 0), stop=(f == 15), skip_group_check=True)
                    last.then_inc(s_wused, 1)
                pe.wait_ge(s_ysb, e + 1)
                for j in range(NT):
                    if j >= 2:
                        pe.wait_ge(s_cbout, e * NT + j)
                    for h in range(2):
                        last = mm(ps[:, 2 * (j % 2) + h, :], giveT[64 * h:64 * h + 64, P * j:P * j + P],
                                  ysb[64 * h:64 * h + 64, :], start=True, stop=True)
                    last.then_inc(s_cb, 1)


_INS = ['x', 'c', 'w_ada', 'b_ada', 'norm1_g', 'w_in', 'q_norm_g', 'k_norm_g', 'na_rpb', 'w_branch_na', 'w_branch_gqa',
        'w_out', 'norm2_g', 'w_router', 'w_exp_gate', 'w_exp_up', 'w_exp_down', 'final_g']
_STACKED = {'w_ada', 'w_in', 'w_branch_na', 'w_branch_gqa', 'w_out', 'w_router', 'w_exp_gate', 'w_exp_up', 'w_exp_down'}


def _constants(np):
    cols, rows, hd = 64, 8, 64
    out = np.zeros((128, 4 * 128 + 768), np.float32)
    out[:, 0:128] = np.eye(128)
    out[:, 128:256] = np.arange(128) % 64 + 1
    half = hd // 2
    inv = np.float32(10000.0) ** (-np.arange(0, half, 2, dtype=np.float32) / np.float32(half))
    t = np.arange(cols * rows)
    col, row = (t // rows).astype(np.float32), (t % rows).astype(np.float32)
    ang = np.concatenate([row[:, None] * inv[None], col[:, None] * inv[None]], axis=-1).astype(np.float32)
    for i, f in ((256, np.cos), (384, np.sin)):
        out[:, i:i + 128] = f(ang).reshape(4, 128, half).transpose(1, 0, 2).reshape(128, 128)
    for v, (c0, k0) in enumerate(((16, 8), (0, 0), (48, 40))):
        q = c0 + np.arange(128) // rows
        start = np.clip(q - 8, 0, cols - 16)
        k = k0 + np.arange(256) // rows
        ok = (k[None] >= start[:, None]) & (k[None] < start[:, None] + 16)
        out[:, 512 + 256 * v:768 + 256 * v] = np.where(ok, 0.0, -1e30)
    return out


def kernel(**inputs):
    import numpy as _np
    import concourse.bacc as _bacc
    from concourse import mybir as _mybir
    from concourse.bass_utils import run_bass_kernel_spmd as _run

    nc = _bacc.Bacc("TRN2", target_bir_lowering=False, num_devices=1)
    arrays, args = {}, []
    for name in _INS + ['consts']:
        a = _constants(_np) if name == 'consts' else _np.asarray(inputs[name])
        if name in _STACKED:
            a = a.reshape(a.shape[1:])
        if name == 'na_rpb':
            a = _np.pad(a[0][:, ::-1].transpose(1, 0, 2), ((0, 0), (0, 0), (8, 8)))
        a = _np.ascontiguousarray(a)
        arrays[f"in_{name}"] = a
        args.append(nc.dram_tensor(f"in_{name}", a.shape, _mybir.dt.from_np(a.dtype), kind="ExternalInput").ap())
    out = nc.dram_tensor("out_0", inputs['x'].shape, _mybir.dt.float32, kind="ExternalOutput").ap()
    encoder_block(nc, *args, out)
    r = _run(nc, [arrays], core_ids=[0])
    return r.results[0]["out_0"]
```

```python
import concourse.bass as bass
from concourse import mybir
from contextlib import ExitStack


def encoder_block(nc, x, c, w_ada, b_ada, norm1_g, w_in, q_norm_g, k_norm_g, na_rpb, w_branch_na, w_branch_gqa,
                  w_out, norm2_g, w_router, w_exp_gate, w_exp_up, w_exp_down, final_g, consts, out):
    f32 = mybir.dt.float32
    f32r = mybir.dt.float32r
    ALU = mybir.AluOpType
    ACT = mybir.ActivationFunctionType
    X = mybir.AxisListType.X

    P = 128
    T, D = x.shape[1], x.shape[2]
    COLS = 64
    ROWS = T // COLS
    NT = T // P
    KD = D // P
    H, HD = 8, 64
    NH = H * HD
    E = w_router.shape[1]
    F = w_exp_gate.shape[2]
    CAP = 2 * T // E
    EPS = 1e-6
    QS = HD ** -0.5
    B = 512

    TILE = 4096
    NSLOT = 8
    N_FRONT = 13
    T_KV, T_GATE, T_BR, T_OUT = 4, 5, 9, 11
    f_slot = lambda m: m % 2 if m < T_OUT else 3 + m - T_OUT
    uses_of = lambda m: m // 2 + 1 if m < T_OUT else 1
    FRONT_USES = [sum(f_slot(m) == s for m in range(N_FRONT)) for s in range(NSLOT)]
    ET = 12
    eslot = lambda i: i % NSLOT
    NADA = 12

    P_KV, P_GATE, P_BR, P_OUT, N_PIECE = 16, 20, 36, 44, 60
    last_piece = lambda m: (4 * m + 3 if m < T_BR else P_OUT - 1)

    B_X = 0
    B_NA = B_X + KD
    B_K = B_NA + 2 * 16
    B_Q = B_K + 1
    B_YN = B_Q + 4
    B_GQ = B_YN + 4
    B_YG = B_GQ + 2 * 16
    B_X2 = B_YG + 4
    B_AFF = B_X2 + 2 * NT
    B_SLOT = B_AFF + 1

    N_PROJ = 36
    G_QG, G_KV, G_GATE = 12, 16, 20

    NAJ = [(1, 64, 256, 0, 3, 0), (2, 192, 256, 128, 3, 0), (3, 320, 192, 256, 2, 2), (0, 0, 256, 0, 2, 1)]

    ctx = ExitStack()
    with ctx:
        def sb(name, shape, dt=f32):
            return ctx.enter_context(nc.sbuf_tensor(name, shape, dt))

        def sem(name):
            return ctx.enter_context(nc.semaphore(name))

        ring_a = sb("ring_a", [P, 5 * TILE])
        xs = sb("x_sb", [P, NT, D])
        sig = sb("sig", [P, KD, T])
        vy = sb("vy", [P, NT, NH])
        qy = sb("qy", [P, 2, NT, NH])
        bias = sb("bias", [P, H, 32, ROWS])
        bm = sb("bm", [P, 2, 2, 256])
        cst = sb("cst", [P, consts.shape[1]])
        gains = sb("gains", [P, 2, HD])
        wr = sb("wr", [P, KD, E])
        vecs = sb("vecs", [24, P])
        col = sb("col", [P, 6, KD])
        stat = sb("stat", [P, 128])
        rsum = sb("rsum", [P, 64])
        nmax = sb("nmax", [P, 64])
        rinv = sb("rinv", [P, 64])
        aff = sb("aff", [P, NT, E])
        slots = sb("slots", [P, NT, E + 1])
        ones = sb("ones", [P, P])
        nhalf = sb("nhalf", [P, 8])
        grow = sb("grow", [P, 512])
        with ExitStack() as front_only:
            fr = lambda name, shape: front_only.enter_context(nc.sbuf_tensor(name, shape, f32r))
            hth = fr("hth", [P, KD, T])
            htl = fr("htl", [P, KD, T])
            wh = fr("wh", [P, 2, 1024])
            wl = fr("wl", [P, 2, 1024])
        ring_b = sb("ring_b", [P, 3 * TILE])
        slot = lambda s: (ring_a[:, s * TILE:(s + 1) * TILE] if s < 5 else ring_b[:, (s - 5) * TILE:(s - 4) * TILE])

        ident = cst[:, 0:P]
        iota = cst[:, P:2 * P]
        cos = cst[:, 2 * P:3 * P].rearrange("p (j f) -> p j f", j=NT)
        sin = cst[:, 3 * P:4 * P].rearrange("p (j f) -> p j f", j=NT)
        mask = cst[:, 4 * P:4 * P + 768].rearrange("p (v k) -> p v k", v=3)
        n1c, n2c, a1, s1, a2, s2 = (col[:, i, :] for i in range(6))

        r2, r3, r4 = slot(2), slot(3), slot(4)
        hT = r2.rearrange("p (k t) -> p k t", k=KD)
        qk = r2.rearrange("p (b t) -> p b t", b=8)
        sigb = r2.rearrange("p (b t) -> p b t", b=8)
        pb = r3[:, 0:2048].rearrange("p (u k) -> p u k", u=4)
        ssb = r3[:, 2048:2560].rearrange("p (u k) -> p u k", u=2)
        ptb = r3[:, 2560:3584].rearrange("p (u k) -> p u k", u=2)
        qt = r4[:, 0:2048].rearrange("p (b t) -> p b t", b=4)
        kvg = r4[:, 2048:3072].rearrange("p (j n) -> p j n", j=NT)
        kt = r4[:, 3072:3584]
        flat = lambda a: a.rearrange("p b t -> p (b t)")
        sigf = flat(sig[:, :, :])
        ada_mem = lambda m: (sigf, r3, r4, slot(1))[m if m < 4 else m % 2].rearrange("p (k n) -> p k n", k=2)
        ada_sem = lambda m: s_ada[m if m < 4 else 4 + m % 2]
        ada_count = lambda m: 16 if m < 4 else 16 * (m // 2 - 1)
        qyf = qy[:, :, :, :].rearrange("p a j n -> p (a j n)")
        bmf = bm[:, :, :, :].rearrange("p a b k -> p (a b k)")
        c32 = bmf[:, 0:256].rearrange("p (k r) -> p k r", k=KD)
        adab = bmf[:, 256:768]
        xh = qyf.rearrange("p (j d) -> p j d", j=NT)
        adar = vy[:, 0:2, :]
        braw = qyf[:, 0:2048].rearrange("p (r h c) -> p r h c", h=H, r=ROWS)
        rt = sigf[:, 3072:4096]
        ytok = qy[:, 1, :, :]
        ytn = vy
        biasf = bias[:, :, :, :].rearrange("p h c r -> p (h c r)")
        gate1 = biasf[:, 0:D]
        fing = biasf[:, D:2 * D]
        gate2 = bmf[:, 0:512]
        xh2 = sigf.rearrange("p (j d) -> p j d", j=NT)
        h2t = qyf.rearrange("p (k t) -> p k t", k=KD)
        work, cum, sel, slot_e = (vy[0:E, i, :] for i in range(4))
        onesr = bmf[0:E, 512:1024]
        top8 = rsum[0:E, 0:64]
        act = qyf[:, 0:1024].rearrange("p (g n) -> p g n", g=2)
        silu = qyf[:, 1024:2048].rearrange("p (g n) -> p g n", g=2)
        actT = qyf[:, 2048:3072].rearrange("p (f s) -> p f s", f=16)
        ysb = qyf[:, 3072:3584]
        xin = qyf[:, 3584:4096]
        vf = flat(vy[:, :, :])
        xinT = vf[:, 0:512].rearrange("p (k s) -> p k s", k=KD)
        pick = vf[:, 512:768].rearrange("p (j s) -> p j s", j=NT)
        give = vf[:, 768:1280].rearrange("p (j s) -> p j s", j=NT)
        giveT = vf[:, 1280:1792]

        def piece(p):
            if p < P_KV:
                return [(slot(f_slot(p // 4))[:, 1024 * (p % 4):1024 * (p % 4) + 1024], 0, 1024)]
            if p < P_GATE:
                return [(slot(f_slot(T_KV))[:, 512 * (p % 4):512 * (p % 4) + 512], 0, 512)]
            if p < P_BR:
                w = slot(f_slot(T_GATE + (p - P_GATE) // 4)).rearrange("p (k n) -> p k n", k=KD)
                return [(w[:, :, P * (p % 4):P * (p % 4) + P], 0, 1024)]
            if p < P_OUT:
                b = p - P_BR
                return [(slot(f_slot(T_BR + i)).rearrange("p (k n) -> p k n", k=4)[:, :, P * b:P * b + P],
                         512 * i, 512) for i in range(2)]
            k = (p - P_OUT) % KD
            return [(slot(f_slot(T_OUT + k // 4))[:, 1024 * (k % 4):1024 * (k % 4) + 1024], 0, 1024)]

        def like(buf, src, c0, n):
            v = buf[:, c0:c0 + n]
            return v.rearrange("p (k n) -> p k n", n=P) if len(src.shape) == 3 else v

        tiles_of = lambda p: ([p // 4] if p < P_BR and p % 4 == 0 else [T_BR, T_BR + 1] if p == P_BR
                              else [T_OUT] if p == P_OUT else [T_OUT + 1] if p == P_OUT + 4 else [])

        ps = ctx.enter_context(nc.psum_tensor("ps", [P, 8, B], f32))

        s_const, s_x, s_vec, s_rpb, s_small, s_fing = map(sem, (
            "const_in", "x_in", "vec_in", "rpb_in", "small_in", "fing_in"))
        s_adab = [sem(f"adab_in{g}") for g in range(3)]
        s_w = [sem(f"w_in{s}") for s in range(NSLOT)]
        s_ada = [sem(f"ada_in{s}") for s in range(6)]
        s_hi, s_lo, s_pused = sem("piece_hi"), sem("piece_lo"), sem("piece_used")
        s_h, s_thi, s_ht = sem("h_ready"), sem("activation_hi"), sem("activation_lo")
        s_wused, s_adaused = sem("w_used"), sem("ada_used")
        s_ones, s_xh, s_tdone = sem("ones_ready"), sem("xh_ready"), sem("t_done")
        s_tout = [sem("t_out_even"), sem("t_out_odd")]
        s_vecT, s_ct, s_adasb, s_colps, s_cols, s_bcps, s_bc = map(sem, (
            "vec_t", "c_silu", "ada_sb", "col_ps", "cols_ready", "bc_ps", "bc_ready"))
        s_proj, s_projout = sem("proj_done"), sem("proj_out")
        s_biasr, s_bm, s_z = sem("bias_ready"), sem("bm_ready"), sem("pads_zero")
        s_s, s_sadd, s_nmax, s_p, s_av, s_y = map(sem, ("scores", "scores_biased", "neg_max", "probs", "av", "y_out"))
        s_rope, s_gain = sem("rope_out"), sem("gains_ready")
        s_sg, s_brout, s_op, s_opout, s_xh2 = map(sem, ("sigmoid", "merged", "outproj", "x2_ready", "xh2_ready"))
        s_oread = sem("outproj_read")
        s_log, s_nm2, s_ex, s_aff, s_slot = map(sem, ("logits", "logits_shift", "logits_exp", "aff_ready", "slots_ready"))
        s_dve = sem("dve_chain")
        s_ss, s_sq, s_rstd, s_nhalf = sem("mean_square"), sem("squares"), sem("rstd"), sem("nhalf_ready")
        s_pick, s_gath, s_give, s_xin, s_xt, s_xinT, s_giveT = map(sem, (
            "pick_ready", "gathered", "give_t", "xin_ready", "xin_t", "xin_t_out", "give_t_out"))
        s_silu, s_act, s_at, s_actT, s_ysb, s_cb, s_cbout = map(sem, (
            "silu_done", "act_ready", "act_t", "act_t_out", "y_ready", "combined", "added"))
        s_fin, s_out = sem("final"), sem("stored")

        block = ctx.enter_context(nc.Block())


        x_rows = x[0].rearrange("(r j c) d -> r c j d", r=ROWS, j=NT)

        def ada_src(m):
            g, k2 = m // 4, m % 4
            return w_ada[256 * k2:256 * k2 + 256, 2048 * g:2048 * g + 2048].rearrange("(k p) n -> p k n", p=P)

        b_ada_rows = lambda g: bass.AP(tensor=b_ada.tensor, offset=2048 * g, ap=[[512, 4], [0, 32], [1, 512]])

        @block.sync
        def _(sp):
            for r in range(ROWS):
                sp.dma_start(xs[r:P:ROWS, :, :], x_rows[r]).then_inc(s_x, 16)
            for m in range(4):
                sp.dma_start(ada_mem(m), ada_src(m)).then_inc(ada_sem(m), 16)

            w_in_k = w_in.rearrange("(k p) n -> p k n", p=P)

            def front(m, src, k):
                if m == 1:
                    sp.wait_ge(s_adaused, 4)
                elif T_OUT > m >= 2:
                    sp.wait_ge(s_lo, last_piece(m - 2) + 1)
                sp.dma_start(slot(f_slot(m))[:, 0:k * src.shape[2]].rearrange("p (k n) -> p k n", k=k),
                             src).then_inc(s_w[f_slot(m)], 16)

            for m in range(4):
                front(m, w_in_k[:, :, 512 * m:512 * m + 512], KD)
            front(T_KV, w_in_k[:, :, 2048:2304], KD)
            for g in range(4):
                front(T_GATE + g, w_in_k[:, :, 2304 + 512 * g:2816 + 512 * g], KD)
            for i, w in enumerate((w_branch_na, w_branch_gqa)):
                front(T_BR + i, w.rearrange("(k p) n -> p k n", p=P), 4)
            sp.wait_ge(s_tdone, B_YG + 4)
            for h in range(2):
                front(T_OUT + h, w_out.rearrange("(k p) n -> p k n", p=P)[:, 4 * h:4 * h + 4, :], 4)

            def expert_tile(e, n):
                i = n % ET
                if i < 8:
                    g, up, kh = i // 4, i // 2 % 2, i % 2
                    w = (w_exp_up if up else w_exp_gate)[bass.ds(e, 1), 512 * kh:512 * kh + 512, 1024 * g:1024 * g + 1024]
                else:
                    w = w_exp_down[bass.ds(e, 1), 512 * (i - 8):512 * (i - 8) + 512, :]
                sp.dma_start(slot(eslot(n)).rearrange("p (k n) -> p k n", k=4),
                             w.rearrange("a (k p) n -> p (a k) n", p=P)).then_inc(s_w[eslot(n)], 16)

            for n in range(2 * ET):
                if n == 0:
                    sp.wait_ge(s_lo, P_OUT)
                elif n == 2:
                    sp.wait_ge(s_brout, KD)
                elif n == 3:
                    sp.wait_ge(s_lo, N_PIECE)
                elif n == 5:
                    sp.wait_ge(s_pused, N_PIECE)
                elif n >= NSLOT:
                    sp.wait_ge(s_wused, n - NSLOT + 1)
                expert_tile(n // ET, n)
            with sp.Fori(1, E // 2) as pair:
                for n in range(2 * ET):
                    sp.wait_ge(s_wused, pair * (2 * ET) + (n - NSLOT + 1))
                    expert_tile(pair * 2 + n // ET, n)
            for j in range(NT):
                sp.wait_ge(s_fin, j + 1)
                for r in range(ROWS):
                    sp.dma_start(out[0].rearrange("(r j c) d -> r c j d", r=ROWS, j=NT)[r][:, j, :],
                                 xs[r:P:ROWS, j, :]).then_inc(s_out, 16)
            sp.wait_ge(s_out, 16 * NT * ROWS)

        @block.gpsimd
        def _(pool):
            nc.gpsimd.memset(ones[:, :], 1.0).then_inc(s_ones, 1)
            nc.gpsimd.memset(nhalf[:, :], -0.5).then_inc(s_nhalf, 1)
            n_pow = [0]

            def power(a, n):
                n_pow[0] += 1
                pool.wait_ge(s_ss, n_pow[0])
                nc.gpsimd.tensor_tensor(a, a, nhalf[:, 0:n], ALU.pow).then_inc(s_rstd, 1)

            pool.wait_ge(s_nhalf, 1)
            for j in range(NT):
                power(stat[:, 8 + j:9 + j], 1)
            for m in range(4, NADA):
                pool.wait_ge(s_adaused, m - 3 if m < 6 else m - 1)
                pool.dma_start(ada_mem(m), ada_src(m)).then_inc(ada_sem(m), 16)
                if m == 5:
                    pool.wait_ge(s_adasb, 1)
                    pool.dma_start(adab, b_ada_rows(1)).then_inc(s_adab[1], 16)
                    pool.wait_ge(s_tdone, B_X + KD)
                    RW = 47
                    for cc in range(16):
                        src = bass.AP(tensor=na_rpb.tensor, offset=15 - cc, ap=[[H * RW, ROWS], [RW, H * ROWS], [1, 32]])
                        pool.dma_start(braw[ROWS * cc:ROWS * cc + ROWS].rearrange("p r h c -> p (r h) c"), src).then_inc(s_rpb, 16)
                if m == 9:
                    pool.wait_ge(s_adasb, 2)
                    pool.dma_start(adab, b_ada_rows(2)).then_inc(s_adab[2], 16)
            pool.wait_ge(s_adaused, NADA)
            nc.gpsimd.memset(pb[:, :, 0:64], 0.0).then_inc(s_z, 1)
            nc.gpsimd.memset(pb[:, :, 320:384], 0.0).then_inc(s_z, 1)
            pool.wait_ge(s_adasb, 3)
            pool.wait_ge(s_biasr, 1)
            pool.wait_ge(s_const, 16)
            for d in range(16):
                j, k0, w, kb, nb, v = NAJ[d // 4]
                h = 2 * (d % 4)
                if d >= 2:
                    pool.wait_ge(s_sadd, d - 1)
                wv = 192 if v else 256
                c0 = 8 if v == 1 else 0
                for i in range(2):
                    last = nc.gpsimd.tensor_tensor(bm[:, d % 2, i, 0:wv],
                                            bias[:, h + i, c0:c0 + wv // 8, :].rearrange("p c r -> p (c r)"),
                                            mask[:, v, 0:wv], ALU.add)
                    last.then_inc(s_bm, 1)
                if v == 1:
                    nc.gpsimd.tensor_copy(bm[:, d % 2, :, 192:256],
                                          mask[:, 1, 192:256].unsqueeze(1).broadcast_to([P, 2, 64])).then_inc(s_bm, 1)
                if 1 <= d <= 8:
                    n = 2 if d <= 4 else H
                    power(stat[:, 16:16 + n], n)
            pool.wait_ge(s_sadd, 16)
            pool.wait_ge(s_y, 16)
            pool.dma_start(fing, final_g.rearrange("(a n) -> a n", a=1).partition_broadcast(P)[:, 0, :]).then_inc(s_fing, 16)
            for j in range(2 * NT):
                power(stat[:, 8 + j % NT:9 + j % NT], 1)

        bm_count = lambda d: 2 * (d + 1) + max(0, d - 11)

        @block.scalar
        def _(act_):
            for i, v in enumerate((c, norm1_g, norm2_g)):
                act_.dma_start(vecs[8 * i:8 * i + 8, :], v.rearrange("b (k p) -> (b k) p", p=P)).then_inc(s_vec, 16)
            act_.dma_start(cst[:, :], consts).then_inc(s_const, 16)
            act_.dma_start(adab, b_ada_rows(0)).then_inc(s_adab[0], 16)
            act_.dma_start(gains[:, 0, :], q_norm_g.partition_broadcast(P)[:, 0, :]).then_inc(s_small, 16)
            act_.dma_start(gains[:, 1, :], k_norm_g.partition_broadcast(P)[:, 0, :]).then_inc(s_small, 16)
            act_.dma_start(wr[:, :, :], w_router.rearrange("(k p) e -> p k e", p=P)).then_inc(s_small, 16)

            act_.wait_ge(s_vecT, 1)
            nc.scalar.activation(c32, ps[:, 7, 0:8].unsqueeze(2).broadcast_to([P, KD, 32]), ACT.Silu).then_inc(s_ct, 1)

            copy = lambda o, i: nc.scalar.activation(o, i, ACT.Copy)

            def out_batch(n, dst, view=lambda a: a):
                if n % 2:
                    act_.wait_ge(s_tdone, n + 1)
                    copy(dst, view(ps[:, 4 + n % 2, :])).then_inc(s_tout[1], 1)

            def hi(p):
                for m in tiles_of(p):
                    act_.wait_ge(s_w[f_slot(m)], 16 * uses_of(m))
                if p >= 2:
                    act_.wait_ge(s_pused, p - 1)
                for src, c0, n in piece(p):
                    last = copy(like(wh[:, p % 2, :], src, c0, n), src)
                last.then_inc(s_hi, 1)

            for k in range(KD):
                out_batch(B_X + k, hT[:, k, :])

            def h_hi(k):
                act_.wait_ge(s_h, k + 1)
                copy(hth[:, k, :], hT[:, k, :]).then_inc(s_thi, 1)

            hi(0)
            h_hi(0)
            h_hi(1)
            hi(1)
            for k in range(2, KD):
                h_hi(k)

            def proj_out(n):
                m, b = n // 4, n % 4
                if n < G_GATE and b < 3:
                    act_.wait_ge(s_proj, 3 * m + b + 1)
                elif n < G_GATE:
                    act_.wait_ge(s_pused, 4 * m + 4)
                else:
                    act_.wait_ge(s_pused, P_GATE + n - G_GATE + 1)
                src = ps[:, b if n < G_GATE else 7, :]
                if n < 4:
                    o = nc.scalar.activation(qk[:, n, :], src, ACT.Copy, scale=QS)
                elif n < 8:
                    o = copy(qk[:, n, :], src)
                elif n < G_QG:
                    if b == 0:
                        act_.wait_ge(s_colps, 2)
                    o = copy(vy[:, b, :], src)
                elif n < G_KV:
                    if b == 0:
                        act_.wait_ge(s_biasr, 1)
                    o = copy(qy[:, 0, b, :].rearrange("p (i g d) -> p g i d", g=2, i=4),
                             src.rearrange("p (g i d) -> p g i d", g=2, i=4))
                elif n < G_GATE:
                    o = copy(kvg[:, b, :], src[:, 0:256])
                elif n < G_GATE + KD:
                    if n == G_GATE + 6:
                        act_.wait_ge(s_rope, 8)
                    o = copy(sig[:, n - G_GATE, :], src)
                else:
                    o = copy(sigb[:, n - G_GATE - KD, :], src)
                o.then_inc(s_projout, 1)

            def exps(d):
                for i in range(2):
                    u = 2 * d + i
                    act_.wait_ge(s_nmax, d + 1)
                    if u >= 4:
                        act_.wait_ge(s_tdone, (B_NA if d < 18 else B_GQ) + (u - 4 if d < 18 else u - 36) + 1)
                    else:
                        act_.wait_ge(s_z, 2)
                    if d < 16:
                        j, k0, w, kb, nb, v = NAJ[d // 4]
                        o, s = pb[:, u % 4, k0 - kb:k0 - kb + w], ssb[:, i, 0:w]
                    else:
                        o, s = pb[:, u % 4, :], ps[:, 2 * (d % 2) + i, :]
                    nc.scalar.activation(o, s, ACT.Exp, bias=nmax[:, u:u + 1],
                                         accum_out=rsum[:, u:u + 1]).then_inc(s_p, 1)

            def pt_out(d):
                base = B_NA if d < 16 else B_GQ - 32
                for i in range(2):
                    n = base + 2 * d + i
                    if n % 2:
                        act_.wait_ge(s_tdone, n + 1)
                        if d:
                            act_.wait_ge(s_av, d)
                        w = P * NAJ[d // 4][4] if d < 16 else T
                        copy(ptb[:, i, 0:w], ps[:, 4 + n % 2, 0:w]).then_inc(s_tout[1], 1)

            for p in range(1, P_GATE):
                hi(p + 1)
                if p % 4 == 3:
                    for b in range(4):
                        proj_out(p - 3 + b)
            for d in range(18):
                if d < 16:
                    exps(d)
                if d % 2 == 0:
                    hi(P_GATE + d // 2 + 1)
                if 1 <= d <= 16:
                    pt_out(d - 1)
                if d == 17:
                    out_batch(B_K, kt)
                    for j in range(NT):
                        out_batch(B_Q + j, qt[:, :, P * j:P * j + P], lambda a: a.rearrange("p (b t) -> p b t", b=4))
                if d % 2:
                    proj_out(G_GATE + d // 2)

            def y_hi(i):
                act_.wait_ge(s_tout[0], (B_GQ + 1) // 2)
                act_.wait_ge(s_tout[1], B_GQ // 2)
                act_.wait_ge(s_pused, P_BR)
                copy(hth[:, i, :], ytn[:, i, :]).then_inc(s_thi, 1)

            for d in range(16, 33):
                if d < 32:
                    exps(d)
                if d == 16:
                    for i in range(4):
                        out_batch(B_YN + i, ytn[:, i, :])
                if d % 2 == 0 and d <= 30:
                    hi(P_GATE + (d + 2) // 2 + 1)
                if d > 16:
                    pt_out(d - 1)
                if d % 2 and d < 30:
                    proj_out(G_GATE + (d + 2) // 2)
                if d in (30, 31):
                    y_hi(2 * (d - 30))
                    y_hi(2 * (d - 30) + 1)
            for i in range(4):
                act_.wait_ge(s_tdone, B_YG + i + 1)
                copy(hth[:, 4 + i, :], ps[:, 4 + (B_YG + i) % 2, :]).then_inc(s_thi, 1)
            act_.wait_ge(s_projout, N_PROJ)
            for b in range(KD):
                for g in (sig, sigb):
                    nc.scalar.activation(g[:, b, :], g[:, b, :], ACT.Sigmoid).then_inc(s_sg, 1)
                hi(P_BR + 2 + b)

            def merged_hi(k):
                act_.wait_ge(s_pused, P_OUT)
                act_.wait_ge(s_brout, k + 1)
                copy(hth[:, k, :], sig[:, k, :]).then_inc(s_thi, 1)

            for k in range(KD):
                merged_hi(k)
                if k in (3, 5, 7):
                    hi(P_OUT + 2 + (k - 3) // 2)

            def square(j):
                act_.wait_ge(s_opout, j + 1)
                nc.scalar.activation(xh2[:, j, :], xs[:, j, :], ACT.Square, scale=D ** -0.5,
                                     accum_out=stat[:, j:j + 1]).then_inc(s_sq, 1)

            def h2_out(j):
                for i in range(2):
                    n = B_X2 + 2 * j + i
                    if n % 2:
                        act_.wait_ge(s_tdone, n + 1)
                        for k in range(4 * i, 4 * i + 4):
                            last = nc.scalar.activation(h2t[:, k, P * j:P * j + P], ps[:, 4 + n % 2, P * (k % 4):P * (k % 4) + P],
                                                        ACT.Identity, bias=s2[:, k:k + 1], scale=a2[:, k:k + 1])
                        last.then_inc(s_tout[1], 1)

            for p in range(P_OUT + 5, N_PIECE):
                hi(p)
                if p in (P_OUT + 10, P_OUT + 11):
                    square(p - P_OUT - 10)
                if p in (P_OUT + 14, P_OUT + 15):
                    h2_out(p - P_OUT - 14)
            for j in (2, 3):
                square(j)
            for j in (2, 3):
                h2_out(j)
            act_.wait_ge(s_nm2, 1)
            nc.scalar.activation(aff[:, :, :], aff[:, :, :], ACT.Exp).then_inc(s_ex, 1)
            if B_AFF % 2:
                act_.wait_ge(s_tdone, B_AFF + 1)
                copy(work.rearrange("e (r c) -> e r c", c=COLS),
                     ps[0:E, 4 + B_AFF % 2, :].rearrange("e (c r) -> e r c", r=ROWS)).then_inc(s_tout[1], 1)
            if B_SLOT % 2:
                act_.wait_ge(s_tdone, B_SLOT + 1)
                copy(slots[:, :, 0:E], ps[:, 4 + B_SLOT % 2, 0:NT * E].rearrange("p (j e) -> p j e", j=NT)).then_inc(s_tout[1], 1)

            with act_.Fori(0, E) as e:
                act_.wait_ge(s_xt, e + 1)
                for k in range(KD):
                    c0 = P * (k % 4) + CAP * (k // 4)
                    nc.scalar.activation(xinT[:, k, :], ps[:, 5, c0:c0 + CAP], ACT.Identity, bias=s2[:, k:k + 1],
                                         scale=a2[:, k:k + 1]).then_inc(s_xinT, 1)
                for g in range(2):
                    act_.wait_ge(s_wused, e * ET + (4 * g + 2))
                    nc.scalar.activation(silu[:, g, :], ps[:, 2 * g, :], ACT.Silu).then_inc(s_silu, 1)

        @block.vector
        def _(dve):
            chain = [0]

            def link(ins):
                chain[0] += 1
                ins.then_inc(s_dve, 1)
                dve.wait_ge(s_dve, chain[0])

            n_pow = [0]

            def mean_square(j, scratch):
                link(nc.vector.tensor_tensor_reduce(out=scratch[:, j, :], in0=xs[:, j, :], in1=xs[:, j, :], scale=1.0 / D,
                                                    scalar=0.0, op0=ALU.mult, op1=ALU.add, accum_out=stat[:, j:j + 1]))
                nc.vector.tensor_scalar(stat[:, 8 + j:9 + j], stat[:, j:j + 1], EPS, None, ALU.add).then_inc(s_ss, 1)

            def rstd_in():
                n_pow[0] += 1
                dve.wait_ge(s_rstd, n_pow[0])

            def normalise(j, dst, ready):
                rstd_in()
                nc.vector.tensor_scalar(dst[:, j, :], xs[:, j, :], stat[:, 8 + j:9 + j], None, ALU.mult).then_inc(ready, 1)

            dve.wait_ge(s_x, 16 * ROWS)
            for j in range(NT):
                mean_square(j, xh)
            for j in range(NT):
                normalise(j, xh, s_xh)
            dve.wait_ge(s_ct, 1)
            nc.vector.tensor_copy(col[:, 0:2, :], ps[:, 7, 8:24].rearrange("p (v k) -> p v k", v=2))

            def out_batch(n, dst, view=lambda a: a):
                if n % 2 == 0:
                    dve.wait_ge(s_tdone, n + 1)
                    nc.vector.tensor_copy(dst, view(ps[:, 4 + n % 2, :])).then_inc(s_tout[0], 1)

            for k in range(KD):
                out_batch(B_X + k, hT[:, k, :])

            raw = lambda a: a.bitcast(f32)

            def lo(p):
                dve.wait_ge(s_hi, p + 1)
                for src, c0, n in piece(p):
                    last = nc.vector.tensor_tensor(like(wl[:, p % 2, :], src, c0, n), src,
                                                   raw(like(wh[:, p % 2, :], src, c0, n)), ALU.subtract)
                last.then_inc(s_lo, 1)

            n_thi = [0]

            def t_lo(k, src, ready):
                n_thi[0] += 1
                dve.wait_ge(s_thi, n_thi[0])
                nc.vector.tensor_tensor(htl[:, k, :], src, raw(hth[:, k, :]), ALU.subtract).then_inc(ready, 1)

            def ada_rows(g):
                dve.wait_ge(s_adaused, 4 * (g + 1))
                dve.wait_ge(s_adab[g], 16)
                parts = ([(adar[:, 0, :], 0, P)], [(grow[0:64, :], 0, 64), (adar[64:P, 1, :], 64, P)],
                         [(adar[0:64, 1, :], 0, 64), (grow[64:P, :], 64, P)])[g]
                for dst, p0, p1 in parts:
                    last = nc.vector.tensor_tensor(dst, ps[p0:p1, 6, :], adab[p0:p1, :], ALU.add)
                last.then_inc(s_adasb, 1)

            def modulation(n, shift, scale, s, a, gain):
                dve.wait_ge(s_colps, n)
                rows = ps[:, 7, :].rearrange("p (b i r) -> p i b r", b=4, i=4)[:, :, :, 0]
                two = lambda v: v.rearrange("p (i b) -> p i b", i=2)
                link(nc.vector.tensor_copy(two(s), rows[:, shift:shift + 2, :]))
                link(nc.vector.scalar_tensor_tensor(out=two(a), in0=rows[:, scale:scale + 2, :], scalar=1.0,
                                                    in1=two(gain), op0=ALU.add, op1=ALU.mult))
                nc.vector.tensor_copy(stat[:, 60:61], a[:, 0:1]).then_inc(s_cols, 1)

            ada_rows(0)
            modulation(1, 0, 2, s1, a1, n1c)
            dve.wait_ge(s_tout[1], KD // 2)

            def modulate(k):
                nc.vector.tensor_scalar(hT[:, k, :], hT[:, k, :], a1[:, k:k + 1], s1[:, k:k + 1], ALU.mult,
                                        ALU.add).then_inc(s_h, 1)

            modulate(0)
            modulate(1)
            lo(0)
            for k in range(KD):
                if k + 2 < KD:
                    modulate(k + 2)
                if k == 2:
                    lo(1)
                t_lo(k, hT[:, k, :], s_ht)
            dve.wait_ge(s_rpb, 16 * 16)
            lo(2)
            nc.vector.tensor_copy(bias[:, :, :, :].rearrange("p h c r -> p r h c"), braw[:, ::-1, :, :]).then_inc(s_biasr, 1)
            lo(3)
            dve.wait_ge(s_small, 48)
            nc.vector.tensor_scalar(gains[:, 1, :], gains[:, 1, :], HD ** 0.5, None, ALU.mult).then_inc(s_gain, 1)
            for p in range(4, P_GATE + 1):
                lo(p)
                if p == 5:
                    ada_rows(1)
                if p == 9:
                    ada_rows(2)
                if p == 10:
                    modulation(2, 2, 0, s2, a2, n2c)

            def rope_of(r):
                j, nh = r % NT, 2 if r < NT else H
                src = (kvg[:, j, 0:P] if r < NT else qy[:, 0, j, :]).rearrange("p (h d) -> p h d", h=nh)
                return j, nh, src, rt[:, 0:nh * HD].rearrange("p (h d) -> p h d", h=nh), stat[:, 16:16 + nh]

            def rope_squares(r):
                j, nh, src, tmp, st = rope_of(r)
                link(nc.vector.tensor_tensor(tmp, src, src, ALU.mult))
                link(nc.vector.tensor_reduce(out=st, in_=tmp, axis=X, op=ALU.add))
                nc.vector.tensor_scalar(st, st, HD * EPS, None, ALU.add).then_inc(s_ss, 1)

            def rope_rotate(r):
                j, nh, src, tmp, st = rope_of(r)
                gain = gains[:, 1 if r < NT else 0, :]
                t2 = rt[:, 512:512 + nh * HD // 2].rearrange("p (h d) -> p h d", h=nh)
                t3 = rt[:, 768:768 + nh * HD // 2].rearrange("p (h d) -> p h d", h=nh)
                rstd_in()
                link(nc.vector.tensor_tensor(tmp, src, st.unsqueeze(2).broadcast_to([P, nh, HD]), ALU.mult))
                link(nc.vector.tensor_tensor(tmp, tmp, gain.unsqueeze(1).broadcast_to([P, nh, HD]), ALU.mult))
                even, odd = tmp[:, :, 0:HD:2], tmp[:, :, 1:HD:2]
                cj = cos[:, j, :].unsqueeze(1).broadcast_to([P, nh, HD // 2])
                sj = sin[:, j, :].unsqueeze(1).broadcast_to([P, nh, HD // 2])
                nc.vector.tensor_tensor(t2, even, cj, ALU.mult)
                link(nc.vector.tensor_tensor(t3, odd, sj, ALU.mult))
                link(nc.vector.tensor_tensor(src[:, :, 0:HD:2], t2, t3, ALU.subtract))
                nc.vector.tensor_tensor(t2, even, sj, ALU.mult)
                link(nc.vector.tensor_tensor(t3, odd, cj, ALU.mult))
                nc.vector.tensor_tensor(src[:, :, 1:HD:2], t2, t3, ALU.add).then_inc(s_rope, 1)

            def softmax(d):
                if d < 16:
                    j, k0, w, kb, nb, v = NAJ[d // 4]
                    dve.wait_ge(s_s, 2 * d + 2)
                    dve.wait_ge(s_bm, bm_count(d))
                    if d:
                        dve.wait_ge(s_p, 2 * d)
                    nc.vector.tensor_tensor(ssb[:, :, 0:w], ps[:, 2 * (d % 2):2 * (d % 2) + 2, 0:w],
                                            bm[:, d % 2, :, 0:w], ALU.add).then_inc(s_sadd, 1)
                    dve.wait_ge(s_sadd, d + 1)
                    src = ssb[:, :, 0:w]
                else:
                    dve.wait_ge(s_s, 2 * d + 2)
                    src = ps[:, 2 * (d % 2):2 * (d % 2) + 2, :]
                nc.vector.tensor_reduce(out=nmax[:, 2 * d:2 * d + 2], in_=src, axis=X, op=ALU.max,
                                        negate=True).then_inc(s_nmax, 1)

            def pt_out(d):
                base = B_NA if d < 16 else B_GQ - 32
                for i in range(2):
                    n = base + 2 * d + i
                    if n % 2 == 0:
                        dve.wait_ge(s_tdone, n + 1)
                        if d:
                            dve.wait_ge(s_av, d)
                        w = P * NAJ[d // 4][4] if d < 16 else T
                        nc.vector.tensor_copy(ptb[:, i, 0:w], ps[:, 4, 0:w]).then_inc(s_tout[0], 1)

            def y_out(d):
                dve.wait_ge(s_p, 2 * d + 2)
                link(nc.vector.reciprocal(rinv[:, 2 * d:2 * d + 2], rsum[:, 2 * d:2 * d + 2]))
                dve.wait_ge(s_av, d + 1)
                if d < 16:
                    j, h, step = NAJ[d // 4][0], 2 * (d % 4), 1
                else:
                    j, h, step = (d - 16) // 4, d % 4, 4
                    if d == 16:
                        dve.wait_ge(s_tdone, B_YN + 4)
                dst = ytok[:, j, :].rearrange("p (h d) -> p h d", h=H)[:, h:h + step + 1:step, :]
                nc.vector.tensor_tensor(dst, ps[:, 6, 0:P].rearrange("p (h d) -> p h d", h=2),
                                        rinv[:, 2 * d:2 * d + 2].unsqueeze(2).broadcast_to([P, 2, HD]),
                                        ALU.mult).then_inc(s_y, 1)

            dve.wait_ge(s_gain, 1)
            dve.wait_ge(s_projout, G_GATE)
            for d in range(18):
                if d < 16:
                    softmax(d)
                if d % 2 == 0:
                    lo(P_GATE + d // 2 + 1)
                if d == 17:
                    out_batch(B_K, kt)
                    for j in range(NT):
                        out_batch(B_Q + j, qt[:, :, P * j:P * j + P], lambda a: a.rearrange("p (b t) -> p b t", b=4))
                if d >= 2:
                    y_out(d - 2)
                if 1 <= d <= 8:
                    rope_rotate(d - 1)
                if d < 8:
                    rope_squares(d)
                if 1 <= d <= 16:
                    pt_out(d - 1)
            for d in range(16, 34):
                if d < 32:
                    softmax(d)
                if d == 16:
                    for i in range(4):
                        out_batch(B_YN + i, ytn[:, i, :])
                if d % 2 == 0 and d <= 30:
                    lo(P_GATE + (d + 2) // 2 + 1)
                if 17 <= d <= 32:
                    pt_out(d - 1)
                if d >= 18:
                    y_out(d - 2)
                if d in (31, 32):
                    for i in (2 * (d - 31), 2 * (d - 31) + 1):
                        t_lo(i, ytn[:, i, :], s_ht)
            for i in range(4):
                n = B_YG + i
                t_lo(4 + i, ps[:, 4 + n % 2, :], s_tout[n % 2])
            dve.wait_ge(s_bcps, 1)
            dve.wait_ge(s_bm, bm_count(15))
            nc.vector.tensor_copy(gate1, ps[:, 2:4, :].rearrange("p a n -> p (a n)")).then_inc(s_bc, 1)
            nc.vector.tensor_copy(gate2, ps[:, 7, :]).then_inc(s_bc, 1)

            for b in range(KD):
                q = 2 * (b % 2)
                dve.wait_ge(s_sg, 2 * b + 2)
                dve.wait_ge(s_pused, P_BR + b + 1)
                nc.vector.tensor_tensor(sig[:, b, :], sig[:, b, :], ps[:, q, :], ALU.mult)
                link(nc.vector.tensor_tensor(sigb[:, b, :], sigb[:, b, :], ps[:, q + 1, :], ALU.mult))
                nc.vector.tensor_tensor(sig[:, b, :], sig[:, b, :], sigb[:, b, :], ALU.add).then_inc(s_brout, 1)
                lo(P_BR + 2 + b)
            for k in range(KD):
                t_lo(k, sig[:, k, :], s_ht)
                if k in (3, 5, 7):
                    lo(P_OUT + 2 + (k - 3) // 2)

            def residual(j):
                q = (0, 2, 6, 0)[j]
                if j % 2 == 0:
                    dve.wait_ge(s_op, j // 2 + 1)
                else:
                    dve.wait_ge(s_pused, P_OUT + KD * (j // 2 + 1))
                nc.vector.tensor_tensor(xh2[:, j, :], ps[:, q:q + 2, :].rearrange("p a n -> p (a n)"), gate1,
                                        ALU.mult).then_inc(s_oread, 1)
                dve.wait_ge(s_oread, j + 1)
                nc.vector.tensor_tensor(xs[:, j, :], xs[:, j, :], xh2[:, j, :], ALU.add).then_inc(s_opout, 1)

            def add_eps(j):
                dve.wait_ge(s_sq, j + 1)
                nc.vector.tensor_scalar(stat[:, 8 + j:9 + j], stat[:, j:j + 1], EPS, None, ALU.add).then_inc(s_ss, 1)

            def h2_out(j):
                for i in range(2):
                    n = B_X2 + 2 * j + i
                    if n % 2 == 0:
                        dve.wait_ge(s_tdone, n + 1)
                        for k in range(4 * i, 4 * i + 4):
                            last = nc.vector.tensor_scalar(h2t[:, k, P * j:P * j + P], ps[:, 4 + n % 2, P * (k % 4):P * (k % 4) + P],
                                                           a2[:, k:k + 1], s2[:, k:k + 1], ALU.mult, ALU.add)
                        last.then_inc(s_tout[0], 1)

            after = {9: lambda: residual(0), 10: lambda: residual(1), 11: lambda: (add_eps(0), normalise(0, xh2, s_xh2), add_eps(1)),
                     12: lambda: normalise(1, xh2, s_xh2), 14: lambda: h2_out(0), 15: lambda: h2_out(1)}
            for p in range(P_OUT + 5, N_PIECE):
                lo(p)
                if p - P_OUT in after:
                    after[p - P_OUT]()
            for j in (2, 3):
                residual(j)
            for j in (2, 3):
                add_eps(j)
                normalise(j, xh2, s_xh2)
            for j in (2, 3):
                h2_out(j)
            dve.wait_ge(s_log, 1)
            lg = ps[:, 3, 0:NT * E].rearrange("p (j e) -> p j e", j=NT)
            bce = lambda a: a.unsqueeze(2).broadcast_to([P, NT, E])
            link(nc.vector.tensor_reduce(out=stat[:, 48:52], in_=lg, axis=X, op=ALU.max))
            nc.vector.tensor_tensor(aff[:, :, :], lg, bce(stat[:, 48:52]), ALU.subtract).then_inc(s_nm2, 1)
            dve.wait_ge(s_ex, 1)
            link(nc.vector.tensor_reduce(out=stat[:, 52:56], in_=aff[:, :, :], axis=X, op=ALU.add))
            link(nc.vector.reciprocal(stat[:, 56:60], stat[:, 52:56]))
            nc.vector.tensor_tensor(aff[:, :, :], aff[:, :, :], bce(stat[:, 56:60]), ALU.mult).then_inc(s_aff, 1)
            nc.vector.memset(onesr, 1.0)
            nc.vector.memset(slots[:, :, E:E + 1], 0.0).then_inc(s_cbout, 1)
            if B_AFF % 2 == 0:
                dve.wait_ge(s_tdone, B_AFF + 1)
                link(nc.vector.tensor_copy(work.rearrange("e (r c) -> e r c", c=COLS),
                                           ps[0:E, 4, :].rearrange("e (c r) -> e r c", r=ROWS)))
            else:
                dve.wait_ge(s_tout[1], B_AFF // 2 + 1)
            for r in range(CAP // 8):
                link(nc.vector.max(out=top8[:, 8 * r:8 * r + 8], in_=work))
                link(nc.vector.match_replace(out=work, in_to_replace=top8[:, 8 * r:8 * r + 8], in_values=work,
                                             imm_value=-1.0))
            link(nc.vector.tensor_scalar(sel, work, 0.0, None, ALU.is_lt))
            link(nc.vector.tensor_tensor_scan(out=cum, data0=onesr, data1=sel, initial=0.0, op0=ALU.mult, op1=ALU.add))
            nc.vector.tensor_tensor(slot_e.rearrange("e (c r) -> e r c", r=ROWS), cum.rearrange("e (r c) -> e r c", c=COLS),
                                    sel.rearrange("e (r c) -> e r c", c=COLS), ALU.mult).then_inc(s_slot, 1)
            if B_SLOT % 2 == 0:
                dve.wait_ge(s_tdone, B_SLOT + 1)
                nc.vector.tensor_copy(slots[:, :, 0:E], ps[:, 4, 0:NT * E].rearrange("p (j e) -> p j e", j=NT)).then_inc(s_tout[0], 1)
                dve.wait_ge(s_tout[0], B_SLOT // 2 + 1)
            else:
                dve.wait_ge(s_tout[1], B_SLOT // 2 + 1)

            def one_hots(e, waits=True):
                for j in range(NT):
                    sc, af = slots[:, j, bass.ds(e, 1)], aff[:, j, bass.ds(e, 1)]
                    nc.vector.tensor_scalar(pick[:, j, :], iota[:, 0:CAP], sc, None, ALU.is_equal)
                    last = nc.vector.tensor_scalar(give[:, j, :], iota, sc, af, ALU.is_equal, ALU.mult)
                last.then_inc(s_pick, 1)

            one_hots(0)

            def expert(e, more):
                dve.wait_ge(s_gath, e + 1)
                nc.vector.tensor_copy(xin, ps[:, 7, :]).then_inc(s_xin, 1)
                dve.wait_ge(s_give, e + 1)
                nc.vector.tensor_copy(giveT, ps[:, 6, :]).then_inc(s_giveT, 1)
                if more:
                    one_hots(e + 1)
                for g in range(2):
                    dve.wait_ge(s_silu, 2 * e + g + 1)
                    dve.wait_ge(s_wused, e * ET + (4 * g + 4))
                    nc.vector.tensor_tensor(act[:, g, :], silu[:, g, :], ps[:, 2 * g + 1, :], ALU.mult).then_inc(s_act, 1)
                for g in range(2):
                    dve.wait_ge(s_at, 2 * e + g + 1)
                    dst = actT[:, 8 * g:8 * g + 8, :].rearrange("p (h b) s -> p b h s", h=2)
                    nc.vector.tensor_copy(dst, ps[:, 5 + g, :].rearrange("p (b h s) -> p b h s", b=4, h=2)).then_inc(s_actT, 1)
                dve.wait_ge(s_wused, e * ET + ET)
                nc.vector.tensor_tensor(ysb, ps[:, 4, :], gate2, ALU.mult).then_inc(s_ysb, 1)
                for j in range(NT):
                    q = 2 * (j % 2)
                    dve.wait_ge(s_cb, 4 * e + j + 1)
                    nc.vector.tensor_tensor(xs[:, j, :], xs[:, j, :], ps[:, q:q + 2, :].rearrange("p a n -> p (a n)"),
                                            ALU.add).then_inc(s_cbout, 1)

            with dve.Fori(0, E - 1) as e:
                expert(e, True)
            expert(E - 1, False)
            dve.wait_ge(s_cbout, NT * E + 1)
            dve.wait_ge(s_fing, 16)
            def final(j):
                rstd_in()
                nc.vector.scalar_tensor_tensor(out=xs[:, j, :], in0=xs[:, j, :], scalar=stat[:, 8 + j:9 + j], in1=fing,
                                               op0=ALU.mult, op1=ALU.mult).then_inc(s_fin, 1)

            for j in range(NT):
                mean_square(j, xh2)
                if j:
                    final(j - 1)
            final(NT - 1)

        @block.tensor
        def _(pe):
            mm = nc.tensor.matmul

            def split_mm(out, left, right, start, stop):
                (lh, ll), (rh, rl) = left, right
                mm(out, lh, rh, start=start, stop=False)
                mm(out, lh, rl, start=False, stop=False)
                return mm(out, ll, rh, start=False, stop=stop)

            def weights(p, k):
                return [a[:, p % 2, 0:512 if P_KV <= p < P_GATE else 1024].rearrange("p (k n) -> p k n", k=k) for a in (wh, wl)]

            acts = lambda k, c0=0, c1=T: (hth[:, k, c0:c1], htl[:, k, c0:c1])
            cut = lambda w, k, c0, c1: (w[0][:, k, c0:c1], w[1][:, k, c0:c1])

            pe.wait_ge(s_vec, 48)
            pe.wait_ge(s_const, 16)
            nc.tensor.transpose(ps[:, 7, 0:24], vecs[:, :], ident[0:24, 0:24]).then_inc(s_vecT, 1)

            def bank_free(n):
                if n >= 2:
                    pe.wait_ge(s_tout[n % 2], n // 2)

            def batches_out(n):
                pe.wait_ge(s_tout[0], (n + 1) // 2)
                pe.wait_ge(s_tout[1], n // 2)

            def batch(n, src, parts=NT):
                bank_free(n)
                for i in range(parts):
                    last = nc.tensor.transpose(ps[:, 4 + n % 2, P * i:P * i + P], src(i), ident)
                last.then_inc(s_tdone, 1)

            def ada(m):
                g, k2 = m // 4, m % 4
                pe.wait_ge(ada_sem(m), ada_count(m))
                if g and k2 == 0:
                    pe.wait_ge(s_adasb, g)
                for kk in range(2):
                    k = 2 * k2 + kk
                    for i in range(4):
                        last = mm(ps[32 * i:32 * i + 32, 6, :], c32[:, k, :], ada_mem(m)[:, kk, 512 * i:512 * i + 512],
                                  start=(k == 0), stop=(k == KD - 1), skip_group_check=True)
                last.then_inc(s_adaused, 1)

            def columns(v):
                for b in range(4):
                    last = nc.tensor.transpose(ps[:, 7, P * b:P * b + P], adar[:, v, P * b:P * b + P], ident)
                last.then_inc(s_colps, 1)

            pe.wait_ge(s_ct, 1)
            ada(0)
            pe.wait_ge(s_xh, NT)
            for k in range(KD):
                batch(B_X + k, lambda j: xh[:, j, P * k:P * k + P])
                if k == 3:
                    ada(1)
            ada(2)
            ada(3)
            pe.wait_ge(s_adasb, 1)
            columns(0)

            for p in range(P_GATE):
                m, q = p // 4, p % 4
                pe.wait_ge(s_lo, p + 1)
                w = weights(p, 2)
                width = 256 if m == T_KV else 512
                if m == 0:
                    pe.wait_ge(s_ht, 2 * q + 2)
                for b in range(4):
                    if m and q == 0:
                        pe.wait_ge(s_projout, 4 * m - 3 + b)
                    for kk in range(2):
                        k = 2 * q + kk
                        if m < 2:
                            left, right = cut(w, kk, P * b, P * b + P), acts(k)
                        else:
                            left, right = acts(k, P * b, P * b + P), cut(w, kk, 0, width)
                        last = split_mm(ps[:, b, 0:width], left, right, k == 0, k == KD - 1)
                    if q == 3 and b < 3:
                        last.then_inc(s_proj, 1)
                last.then_inc(s_pused, 1)
                if 1 <= p <= 8:
                    ada(3 + p)
                if p == 9:
                    pe.wait_ge(s_adasb, 3)
                    pe.wait_ge(s_cols, 1)
                    columns(1)

            def gates(g, half):
                p = P_GATE + g
                if half == 0:
                    pe.wait_ge(s_lo, p + 1)
                    pe.wait_ge(s_projout, G_GATE + g)
                w = weights(p, KD)
                for k in range(4 * half, 4 * half + 4):
                    last = split_mm(ps[:, 7, :], cut(w, k, 0, P), acts(k), k == 0, k == KD - 1)
                if half:
                    last.then_inc(s_pused, 1)

            def scores(d):
                if d >= 18:
                    pe.wait_ge(s_p, 2 * d - 2)
                elif d >= 2:
                    pe.wait_ge(s_sadd, d - 1)
                for i in range(2):
                    r = slice(HD * i, HD * i + HD)
                    if d < 16:
                        j, k0, w, kb, nb, v = NAJ[d // 4]
                        q, k = qk[r, d % 4, P * j:P * j + P], qk[r, 4 + d % 4, k0:k0 + w]
                    else:
                        j, w = (d - 16) // 4, T
                        q, k = qt[r, d % 4, P * j:P * j + P], kt[r, :]
                    mm(ps[:, 2 * (d % 2) + i, 0:w], q, k, start=True, stop=True).then_inc(s_s, 1)

            def transposes(d):
                base = B_NA if d < 16 else B_GQ - 32
                for i in range(2):
                    u = 2 * d + i
                    n = base + u
                    pe.wait_ge(s_p, u + 1)
                    bank_free(n)
                    nb = NAJ[d // 4][4] if d < 16 else NT
                    for b in range(nb):
                        last = nc.tensor.transpose(ps[:, 4 + n % 2, P * b:P * b + P], pb[:, u % 4, P * b:P * b + P], ident)
                    last.then_inc(s_tdone, 1)

            def weighted(d):
                base = B_NA if d < 16 else B_GQ - 32
                batches_out(base + 2 * d + 2)
                if d:
                    pe.wait_ge(s_y, d)
                for i in range(2):
                    nb = NAJ[d // 4][4] if d < 16 else NT
                    for b in range(nb):
                        if d < 16:
                            v = vy[:, NAJ[d // 4][3] // P + b, HD * (2 * (d % 4) + i):HD * (2 * (d % 4) + i) + HD]
                        else:
                            v = kvg[:, b, P + HD * i:P + HD * i + HD]
                        last = mm(ps[:, 6, HD * i:HD * i + HD], ptb[:, i, P * b:P * b + P], v, start=(b == 0),
                                  stop=(b == nb - 1))
                last.then_inc(s_av, 1)

            pe.wait_ge(s_projout, G_GATE)
            pe.wait_ge(s_cols, 2)
            for d in range(18):
                if d < 16:
                    scores(d)
                if d == 17:
                    pe.wait_ge(s_rope, 8)
                    batch(B_K, lambda j: kvg[:, j, 0:P])
                    for j in range(NT):
                        batch(B_Q + j, lambda b: qy[:, 0, j, P * b:P * b + P])
                if d >= 2:
                    weighted(d - 2)
                gates(d // 2, d % 2)
                if 1 <= d <= 16:
                    transposes(d - 1)
            batches_out(B_YN)
            for d in range(16, 34):
                if d < 32:
                    scores(d)
                if d == 16:
                    pe.wait_ge(s_y, 16)
                    for i in range(4):
                        batch(B_YN + i, lambda j: ytok[:, j, P * i:P * i + P])
                if d >= 18:
                    weighted(d - 2)
                if d < 30:
                    gates((d + 2) // 2, d % 2)
                if 17 <= d <= 32:
                    transposes(d - 1)
            pe.wait_ge(s_y, 32)
            for i in range(4):
                batch(B_YG + i, lambda j: ytok[:, j, P * i:P * i + P])
            pe.wait_ge(s_projout, N_PROJ)
            pe.wait_ge(s_p, 64)
            for i in range(2):
                mm(ps[:, 2 + i, :], ones[32 * i:32 * i + 1, :], grow[32 * i:32 * i + 1, :], start=True, stop=True)
            for h in range(2):
                q = 64 + 32 * h
                last = mm(ps[64 * h:64 * h + 64, 7, :], ones[q:q + 1, 0:64], grow[q:q + 1, :], start=True, stop=True)
            last.then_inc(s_bcps, 1)

            batches_out(B_YG + 4)
            pe.wait_ge(s_ht, KD + 4)
            for b in range(KD):
                pe.wait_ge(s_lo, P_BR + b + 1)
                if b == 1:
                    pe.wait_ge(s_bc, 2)
                if b >= 2:
                    pe.wait_ge(s_brout, b - 1)
                w = weights(P_BR + b, KD)
                for k in range(KD):
                    last = split_mm(ps[:, 2 * (b % 2) + k // 4, :], cut(w, k, 0, P), acts(k), k % 4 == 0, k % 4 == 3)
                last.then_inc(s_pused, 1)

            def h2_transposes(j):
                pe.wait_ge(s_xh2, j + 1)
                for i in range(2):
                    batch(B_X2 + 2 * j + i, lambda k: xh2[:, j, P * (4 * i + k):P * (4 * i + k) + P])

            def logits(j):
                batches_out(B_X2 + 2 * j + 2)
                for k in range(KD):
                    last = mm(ps[:, 3, E * j:E * j + E], h2t[:, k, P * j:P * j + P], wr[:, k, :], start=(k == 0),
                              stop=(k == KD - 1))
                return last

            pe.wait_ge(s_brout, KD)
            for t in range(2):
                for k in range(KD):
                    p = P_OUT + KD * t + k
                    pe.wait_ge(s_lo, p + 1)
                    if t == 0:
                        pe.wait_ge(s_ht, KD + 4 + k + 1)
                    w = weights(p, 1)
                    for j in (2 * t, 2 * t + 1):
                        if j == 3 and k == 0:
                            pe.wait_ge(s_oread, 1)
                        for h in range(2):
                            last = split_mm(ps[:, (0, 2, 6, 0)[j] + h, :], acts(k, P * j, P * j + P),
                                            cut(w, 0, 512 * h, 512 * h + 512), k == 0, k == KD - 1)
                        if k == KD - 1 and j == 2 * t:
                            last.then_inc(s_op, 1)
                    last.then_inc(s_pused, 1)
                    if p in (P_OUT + 13, P_OUT + 14):
                        h2_transposes(p - P_OUT - 13)
            pe.wait_ge(s_opout, 2)
            logits(0)
            logits(1)
            h2_transposes(2)
            h2_transposes(3)
            logits(2)
            logits(3).then_inc(s_log, 1)
            pe.wait_ge(s_aff, 1)
            bank_free(B_AFF)
            for j in range(NT):
                last = nc.tensor.transpose(ps[0:E, 4 + B_AFF % 2, P * j:P * j + P], aff[:, j, :], ident)
            last.then_inc(s_tdone, 1)
            pe.wait_ge(s_slot, 1)
            bank_free(B_SLOT)
            for j in range(NT):
                last = nc.tensor.transpose(ps[:, 4 + B_SLOT % 2, E * j:E * j + E], slot_e[:, P * j:P * j + P],
                                           ident[0:E, 0:E])
            last.then_inc(s_tdone, 1)

            def tile_in(pair, half, i):
                n = ET * half + i
                s = eslot(n)
                pe.wait_ge(s_w[s], pair * (16 * 2 * ET // NSLOT) + 16 * (FRONT_USES[s] + n // NSLOT + 1))
                return slot(s).rearrange("p (k n) -> p k n", k=4)

            def expert(pair, half):
                e = pair * 2 + half
                pe.wait_ge(s_pick, e + 1)
                for j in range(NT):
                    for h in range(2):
                        last = mm(ps[64 * h:64 * h + 64, 7, :], pick[:, j, :], xh2[:, j, 512 * h:512 * h + 512],
                                  start=(j == 0), stop=(j == NT - 1), skip_group_check=True)
                last.then_inc(s_gath, 1)
                for j in range(NT):
                    last = nc.tensor.transpose(ps[:, 6, P * j:P * j + P], give[:, j, :], ident)
                last.then_inc(s_give, 1)
                pe.wait_ge(s_xin, e + 1)
                for b in range(4):
                    last = nc.tensor.transpose(ps[:, 5, P * b:P * b + P], xin[:, P * b:P * b + P], ident)
                last.then_inc(s_xt, 1)
                pe.wait_ge(s_xinT, (e + 1) * KD)
                pe.wait_ge(s_cbout, e * NT + 1)
                for g in range(2):
                    for up in range(2):
                        for kh in range(2):
                            w = tile_in(pair, half, 4 * g + 2 * up + kh)
                            for kk in range(4):
                                for h in range(2):
                                    last = mm(ps[64 * h:64 * h + 64, 2 * g + up, :], xinT[:, 4 * kh + kk, :],
                                              w[:, kk, 512 * h:512 * h + 512], start=(kh + kk == 0),
                                              stop=(kh + kk == 4), skip_group_check=True)
                            last.then_inc(s_wused, 1)
                for g in range(2):
                    pe.wait_ge(s_act, 2 * e + (g + 1))
                    if g:
                        pe.wait_ge(s_giveT, e + 1)
                    for b in range(4):
                        last = nc.tensor.transpose(ps[:, 5 + g, P * b:P * b + P], act[:, g, P * b:P * b + P], ident)
                    last.then_inc(s_at, 1)
                for i in range(8, 12):
                    if i % 2 == 0:
                        pe.wait_ge(s_actT, 2 * e + (i // 2 - 3))
                    w = tile_in(pair, half, i)
                    for kk in range(4):
                        f = 4 * (i - 8) + kk
                        for h in range(2):
                            last = mm(ps[64 * h:64 * h + 64, 4, :], actT[:, f, :], w[:, kk, 512 * h:512 * h + 512],
                                      start=(f == 0), stop=(f == 15), skip_group_check=True)
                    last.then_inc(s_wused, 1)
                pe.wait_ge(s_ysb, e + 1)
                for j in range(NT):
                    if j >= 2:
                        pe.wait_ge(s_cbout, e * NT + j)
                    for h in range(2):
                        last = mm(ps[:, 2 * (j % 2) + h, :], giveT[64 * h:64 * h + 64, P * j:P * j + P],
                                  ysb[64 * h:64 * h + 64, :], start=True, stop=True)
                    last.then_inc(s_cb, 1)

            with pe.Fori(0, E // 2) as pair:
                expert(pair, 0)
                expert(pair, 1)



_INS = ['x', 'c', 'w_ada', 'b_ada', 'norm1_g', 'w_in', 'q_norm_g', 'k_norm_g', 'na_rpb', 'w_branch_na', 'w_branch_gqa',
        'w_out', 'norm2_g', 'w_router', 'w_exp_gate', 'w_exp_up', 'w_exp_down', 'final_g']
_STACKED = {'w_ada', 'w_in', 'w_branch_na', 'w_branch_gqa', 'w_out', 'w_router', 'w_exp_gate', 'w_exp_up', 'w_exp_down'}


def _constants(np):
    cols, rows, hd = 64, 8, 64
    out = np.zeros((128, 4 * 128 + 768), np.float32)
    out[:, 0:128] = np.eye(128)
    out[:, 128:256] = np.arange(128) % 64 + 1
    half = hd // 2
    inv = np.float32(10000.0) ** (-np.arange(0, half, 2, dtype=np.float32) / np.float32(half))
    t = np.arange(cols * rows)
    col, row = (t // rows).astype(np.float32), (t % rows).astype(np.float32)
    ang = np.concatenate([row[:, None] * inv[None], col[:, None] * inv[None]], axis=-1).astype(np.float32)
    for i, f in ((256, np.cos), (384, np.sin)):
        out[:, i:i + 128] = f(ang).reshape(4, 128, half).transpose(1, 0, 2).reshape(128, 128)
    for v, (c0, k0) in enumerate(((16, 8), (0, 0), (48, 40))):
        q = c0 + np.arange(128) // rows
        start = np.clip(q - 8, 0, cols - 16)
        k = k0 + np.arange(256) // rows
        ok = (k[None] >= start[:, None]) & (k[None] < start[:, None] + 16)
        out[:, 512 + 256 * v:768 + 256 * v] = np.where(ok, 0.0, -1e30)
    return out


def kernel(**inputs):
    import numpy as _np
    import concourse.bacc as _bacc
    from concourse import mybir as _mybir
    from concourse.bass_utils import run_bass_kernel_spmd as _run

    nc = _bacc.Bacc("TRN2", target_bir_lowering=False, num_devices=1)
    arrays, args = {}, []
    for name in _INS + ['consts']:
        a = _constants(_np) if name == 'consts' else _np.asarray(inputs[name])
        if name in _STACKED:
            a = a.reshape(a.shape[1:])
        if name == 'na_rpb':
            a = _np.pad(a[0][:, ::-1].transpose(1, 0, 2), ((0, 0), (0, 0), (8, 8)))
        a = _np.ascontiguousarray(a)
        arrays[f"in_{name}"] = a
        args.append(nc.dram_tensor(f"in_{name}", a.shape, _mybir.dt.from_np(a.dtype), kind="ExternalInput").ap())
    out = nc.dram_tensor("out_0", inputs['x'].shape, _mybir.dt.float32, kind="ExternalOutput").ap()
    encoder_block(nc, *args, out)
    r = _run(nc, [arrays], core_ids=[0])
    return r.results[0]["out_0"]
```

```python
import concourse.bass as bass
from concourse import mybir
from contextlib import ExitStack


def encoder_block(nc, x, c, w_ada, b_ada, norm1_g, w_in, q_norm_g, k_norm_g, na_rpb, w_branch_na, w_branch_gqa,
                  w_out, norm2_g, w_router, w_exp_gate, w_exp_up, w_exp_down, final_g, consts, out):
    f32 = mybir.dt.float32
    f32r = mybir.dt.float32r
    ALU = mybir.AluOpType
    ACT = mybir.ActivationFunctionType
    X = mybir.AxisListType.X

    P = 128
    T, D = x.shape[1], x.shape[2]
    COLS = 64
    ROWS = T // COLS
    NT = T // P
    KD = D // P
    H, HD = 8, 64
    NH = H * HD
    E = w_router.shape[1]
    F = w_exp_gate.shape[2]
    CAP = 2 * T // E
    EPS = 1e-6
    QS = HD ** -0.5
    B = 512

    TILE = 4096
    NSLOT = 9
    E_TILE, E_SLOTS = TILE // 2, 2 * NSLOT
    T_KV, T_GATE, T_BR, T_OUT = 4, 5, 9, 11
    f_slot = lambda m: m % 2 if m < T_OUT else 3 + m - T_OUT
    uses_of = lambda m: m // 2 + 1 if m < T_OUT else 1
    ET = 24
    eslot = lambda i: i % E_SLOTS
    GROUP = 3
    NADA = 12

    P_KV, P_GATE, P_BR, P_OUT, N_PIECE = 16, 20, 36, 44, 60
    last_piece = lambda m: (4 * m + 3 if m < T_BR else P_OUT - 1)

    B_X = 0
    B_NA = B_X + KD
    B_K = B_NA + 2 * 16
    B_Q = B_K + 1
    B_YN = B_Q + 4
    B_GQ = B_YN + 4
    B_X2 = B_GQ + 2 * 16 + NT
    gq_batch = lambda u: B_GQ + u + (u >= 30)
    yg_batch = lambda j: B_GQ + 30 if j == 0 else B_GQ + 32 + j
    pt_batch = lambda d, i: B_NA + 2 * d + i if d < 16 else gq_batch(2 * (d - 16) + i)
    B_AFF = B_X2 + 2 * NT
    B_SLOT = B_AFF + 1

    N_PROJ = 36
    G_QG, G_KV, G_GATE = 12, 16, 20

    NAJ = [(1, 64, 256, 0, 3, 0), (2, 192, 256, 128, 3, 0), (3, 320, 192, 256, 2, 2), (0, 0, 256, 0, 2, 1)]

    ctx = ExitStack()
    with ctx:
        def sb(name, shape, dt=f32):
            return ctx.enter_context(nc.sbuf_tensor(name, shape, dt))

        def sem(name):
            return ctx.enter_context(nc.semaphore(name))

        ring_a = sb("ring_a", [P, 5 * TILE])
        xs = sb("x_sb", [P, NT, D])
        sig = sb("sig", [P, KD, T])
        vy = sb("vy", [P, NT, NH])
        qy = sb("qy", [P, 2, NT, NH])
        bias = sb("bias", [P, H, 32, ROWS])
        bm = sb("bm", [P, 2, 2, 256])
        cst = sb("cst", [P, consts.shape[1]])
        gains = sb("gains", [P, 2, HD])
        wr = sb("wr", [P, KD, E])
        vecs = sb("vecs", [24, P])
        col = sb("col", [P, 6, KD])
        stat = sb("stat", [P, 128])
        rsum = sb("rsum", [P, 64])
        nmax = sb("nmax", [P, 64])
        rinv = sb("rinv", [P, 64])
        aff = sb("aff", [P, NT, E])
        slots = sb("slots", [P, NT, E + 1])
        ones = sb("ones", [P, P])
        nhalf = sb("nhalf", [P, 8])
        grow = sb("grow", [P, 512])
        with ExitStack() as front_only:
            fr = lambda name, shape: front_only.enter_context(nc.sbuf_tensor(name, shape, f32r))
            hth = fr("hth", [P, KD, T])
            htl = fr("htl", [P, KD, T])
            wh = fr("wh", [P, 2, 1024])
            wl = fr("wl", [P, 2, 1024])
        ring_b = sb("ring_b", [P, 3 * TILE])
        qyf = qy[:, :, :, :].rearrange("p a j n -> p (a j n)")
        slot = lambda s: (ring_a[:, s * TILE:(s + 1) * TILE] if s < 5 else ring_b[:, (s - 5) * TILE:(s - 4) * TILE]
                          if s < 8 else qyf)
        e_tile = lambda s: slot(s // 2)[:, E_TILE * (s % 2):E_TILE * (s % 2) + E_TILE].rearrange("p (k n) -> p k n", k=2)

        ident = cst[:, 0:P]
        iota = cst[:, P:2 * P]
        cos = cst[:, 2 * P:3 * P].rearrange("p (j f) -> p j f", j=NT)
        sin = cst[:, 3 * P:4 * P].rearrange("p (j f) -> p j f", j=NT)
        mask = cst[:, 4 * P:4 * P + 768].rearrange("p (v k) -> p v k", v=3)
        n1c, n2c, a1, s1, a2, s2 = (col[:, i, :] for i in range(6))

        r2, r3, r4 = slot(2), slot(3), slot(4)
        hT = r2.rearrange("p (k t) -> p k t", k=KD)
        qk = r2.rearrange("p (b t) -> p b t", b=8)
        sigb = r2.rearrange("p (b t) -> p b t", b=8)
        pb = r3[:, 0:2048].rearrange("p (u k) -> p u k", u=4)
        ssb = r3[:, 2048:2560].rearrange("p (u k) -> p u k", u=2)
        ptb = r3[:, 2560:3584].rearrange("p (u k) -> p u k", u=2)
        qt = r4[:, 0:2048].rearrange("p (b t) -> p b t", b=4)
        kvg = r4[:, 2048:3072].rearrange("p (j n) -> p j n", j=NT)
        kt = r4[:, 3072:3584]
        flat = lambda a: a.rearrange("p b t -> p (b t)")
        sigf = flat(sig[:, :, :])
        ADA_MEM = [0, 1, 2, 3, 0, 1, 2, 1, 2, 1, 0, 1]
        ada_mem = lambda m: (sigf, r3, r4, slot(1))[ADA_MEM[m]].rearrange("p (k n) -> p k n", k=2)
        ada_sem = lambda m: s_ada[m if m < 4 else 4 + ADA_MEM[m]]
        ada_count = lambda m: 16 if m < 4 else 16 * ADA_MEM[4:m + 1].count(ADA_MEM[m])
        ada_sum = lambda g: ada_mem(4 * g)[:, 0, :]
        bmf = bm[:, :, :, :].rearrange("p a b k -> p (a b k)")
        c32 = bmf[:, 0:256].rearrange("p (k r) -> p k r", k=KD)
        adab = bmf[:, 256:768]
        xh = qyf.rearrange("p (j d) -> p j d", j=NT)
        adar = (vy[:, 0, :], qy[:, 1, 0, :])
        braw = qyf[:, 0:2048].rearrange("p (r h c) -> p r h c", h=H, r=ROWS)
        rt = r4[:, 0:1024]
        ytok = qy[:, 1, :, :]
        ytn = vy
        biasf = bias[:, :, :, :].rearrange("p h c r -> p (h c r)")
        gate1 = biasf[:, 0:D]
        fing = slot((E * ET // 2) % NSLOT)[:, 0:D]
        gate2 = bmf[:, 0:512]
        xh2 = sigf.rearrange("p (j d) -> p j d", j=NT)
        h2t = qyf.rearrange("p (k t) -> p k t", k=KD)
        work, cum, sel, slot_e = (vy[0:E, i, :] for i in range(4))
        onesr = bmf[0:E, 512:1024]
        top8 = rsum[0:E, 0:64]
        act = biasf[:, 0:1024].rearrange("p (g n) -> p g n", g=2)
        silu = biasf[:, 1024:2048].rearrange("p (g n) -> p g n", g=2)
        actT = cst[:, 2 * P:2 * P + 1024].rearrange("p (f s) -> p f s", f=16)
        ysb = bmf[:, 512:1024]
        xin = grow[:, :]
        vf = flat(vy[:, :, :])
        xinT = vf[:, 0:512].rearrange("p (k s) -> p k s", k=KD)
        pick = vf[:, 512:768].rearrange("p (j s) -> p j s", j=NT)
        give = vf[:, 768:1280].rearrange("p (j s) -> p j s", j=NT)
        giveT = vf[:, 1280:1792]

        def piece(p):
            if p < P_KV:
                return [(slot(f_slot(p // 4))[:, 1024 * (p % 4):1024 * (p % 4) + 1024], 0, 1024)]
            if p < P_GATE:
                return [(slot(f_slot(T_KV))[:, 512 * (p % 4):512 * (p % 4) + 512], 0, 512)]
            if p < P_BR:
                w = slot(f_slot(T_GATE + (p - P_GATE) // 4)).rearrange("p (k n) -> p k n", k=KD)
                return [(w[:, :, P * (p % 4):P * (p % 4) + P], 0, 1024)]
            if p < P_OUT:
                b = p - P_BR
                return [(slot(f_slot(T_BR + i)).rearrange("p (k n) -> p k n", k=4)[:, :, P * b:P * b + P],
                         512 * i, 512) for i in range(2)]
            k = (p - P_OUT) % KD
            return [(slot(f_slot(T_OUT + k // 4))[:, 1024 * (k % 4):1024 * (k % 4) + 1024], 0, 1024)]

        def like(buf, src, c0, n):
            v = buf[:, c0:c0 + n]
            return v.rearrange("p (k n) -> p k n", n=P) if len(src.shape) == 3 else v

        tiles_of = lambda p: ([0] if p == 1 else [p // 4] if 0 < p < P_BR and p % 4 == 0 else [T_BR, T_BR + 1] if p == P_BR
                              else [T_OUT] if p == P_OUT else [T_OUT + 1] if p == P_OUT + 4 else [])

        ps = ctx.enter_context(nc.psum_tensor("ps", [P, 8, B], f32))

        ROPE_AT = [0, 1, 2, 3, 5, 8, 11, 14]
        SCALE_AT = [1, 2, 3, 4, 6, 9, 12, 15]
        ROTATE_AT = [1, 2, 3, 4, 7, 10, 13, 16]

        s_const, s_ident, s_vec, s_rpb, s_small, s_fing = map(sem, (
            "const_in", "ident_in", "vec_in", "rpb_in", "small_in", "fing_in"))
        s_adab = [sem(f"adab_in{g}") for g in range(3)]
        s_x = [sem(f"x_in{j}") for j in range(NT)]
        s_w = [sem(f"w_in{s}") for s in range(5)]
        s_e = [sem(f"e_in{s}") for s in range(E_SLOTS)]
        s_ada = [sem(f"ada_in{s}") for s in range(8)]
        s_w0 = sem("w_in0_first")
        s_hi, s_lo, s_pused = sem("piece_hi"), sem("piece_lo"), sem("piece_used")
        s_h, s_thi, s_ht = sem("h_ready"), sem("activation_hi"), sem("activation_lo")
        s_wused, s_adaused, s_red = sem("w_used"), sem("ada_used"), sem("ada_reduced")
        s_ones, s_xh, s_tdone = sem("ones_ready"), sem("xh_ready"), sem("t_done")
        s_tout = [sem("t_out_even"), sem("t_out_odd")]
        s_vecT, s_ct, s_adasb, s_colps, s_cols, s_bcps, s_bc = map(sem, (
            "vec_t", "c_silu", "ada_sb", "col_ps", "cols_ready", "bc_ps", "bc_ready"))
        s_proj, s_projout = sem("proj_done"), sem("proj_out")
        s_biasr, s_bm, s_z = sem("bias_ready"), sem("bm_ready"), sem("pads_zero")
        s_s, s_sadd, s_nmax, s_p, s_av, s_y = map(sem, ("scores", "scores_biased", "neg_max", "probs", "av", "y_out"))
        s_rope, s_gain = sem("rope_out"), sem("gains_ready")
        s_sg, s_brout, s_op, s_opout, s_xh2 = map(sem, ("sigmoid", "merged", "outproj", "x2_ready", "xh2_ready"))
        s_gready = sem("give_ready")
        s_oread, s_bread = sem("outproj_read"), sem("branch_read")
        s_log, s_nm2, s_ex, s_aff, s_slot = map(sem, ("logits", "logits_shift", "logits_exp", "aff_ready", "slots_ready"))
        s_dve = sem("dve_chain")
        s_ss, s_sq, s_rstd, s_nhalf = sem("mean_square"), sem("squares"), sem("rstd"), sem("nhalf_ready")
        s_pick, s_gath, s_give, s_xin, s_xt, s_xinT, s_giveT = map(sem, (
            "pick_ready", "gathered", "give_t", "xin_ready", "xin_t", "xin_t_out", "give_t_out"))
        s_silu, s_act, s_at, s_actT, s_ysb, s_cb, s_cbout = map(sem, (
            "silu_done", "act_ready", "act_t", "act_t_out", "y_ready", "combined", "added"))
        s_fin, s_out = sem("final"), sem("stored")

        block = ctx.enter_context(nc.Block())

        grid_tile = lambda a, j: bass.AP(tensor=a.tensor, offset=j * (COLS // NT) * D,
                                         ap=[[D, COLS // NT], [COLS * D, ROWS], [1, D]])

        def ada_src(m):
            g, k2 = m // 4, m % 4
            return w_ada[256 * k2:256 * k2 + 256, 2048 * g:2048 * g + 2048].rearrange("(k p) n -> p k n", p=P)

        b_ada_rows = lambda g: bass.AP(tensor=b_ada.tensor, offset=2048 * g, ap=[[512, 4], [0, 32], [1, 512]])

        @block.sync
        def _(sp):
            for j in range(NT):
                sp.dma_start(xs[:, j, :], grid_tile(x, j)).then_inc(s_x[j], 16)
            for m in range(3):
                sp.dma_start(ada_mem(m), ada_src(m)).then_inc(ada_sem(m), 16)
            for kk in range(2):
                sp.dma_start(ada_mem(3)[:, kk, :], ada_src(3)[:, kk, :]).then_inc(s_ada[7] if kk else ada_sem(3), 16)

            w_in_k = w_in.rearrange("(k p) n -> p k n", p=P)

            def front(m, src, k):
                if m == 1:
                    sp.wait_ge(s_adaused, 4)
                elif T_OUT > m >= 2:
                    sp.wait_ge(s_lo, last_piece(m - 2) + 1)
                sp.dma_start(slot(f_slot(m))[:, 0:k * src.shape[2]].rearrange("p (k n) -> p k n", k=k),
                             src).then_inc(s_w[f_slot(m)], 16)

            for k0, k1, loaded in ((0, 2, s_w0), (2, KD, s_w[0])):
                sp.dma_start(slot(0)[:, 512 * k0:512 * k1].rearrange("p (k n) -> p k n", n=512),
                             w_in_k[:, k0:k1, 0:512]).then_inc(loaded, 16)
            for m in range(1, 4):
                front(m, w_in_k[:, :, 512 * m:512 * m + 512], KD)
            front(T_KV, w_in_k[:, :, 2048:2304], KD)
            for g in range(4):
                front(T_GATE + g, w_in_k[:, :, 2304 + 512 * g:2816 + 512 * g], KD)
            for i, w in enumerate((w_branch_na, w_branch_gqa)):
                front(T_BR + i, w.rearrange("(k p) n -> p k n", p=P), 4)
            sp.wait_ge(s_tdone, B_X2)
            for h in range(2):
                front(T_OUT + h, w_out.rearrange("(k p) n -> p k n", p=P)[:, 4 * h:4 * h + 4, :], 4)

            def expert_tile(e, n):
                i = n % ET
                if i < 16:
                    g, up, k2 = i // 8, i // 4 % 2, i % 4
                    w = (w_exp_up if up else w_exp_gate)[bass.ds(e, 1), 256 * k2:256 * k2 + 256, 1024 * g:1024 * g + 1024]
                else:
                    w = w_exp_down[bass.ds(e, 1), 256 * (i - 16):256 * (i - 16) + 256, :]
                sp.dma_start(e_tile(eslot(n)), w.rearrange("a (k p) n -> p (a k) n", p=P)).then_inc(s_e[eslot(n)], 16)

            for n in range(GROUP * ET):
                if n == 0:
                    sp.wait_ge(s_lo, P_OUT)
                elif n == 2 * 2:
                    sp.wait_ge(s_brout, KD)
                elif n == 2 * 3:
                    sp.wait_ge(s_lo, N_PIECE)
                elif n == 2 * 5:
                    sp.wait_ge(s_pused, N_PIECE)
                elif n == 2 * 8:
                    sp.wait_ge(s_log, 1)
                elif n >= E_SLOTS:
                    sp.wait_ge(s_wused, n - E_SLOTS + 1)
                expert_tile(n // ET, n)
            with sp.Fori(1, E // GROUP) as group:
                for n in range(GROUP * ET):
                    sp.wait_ge(s_wused, group * (GROUP * ET) + (n - E_SLOTS + 1))
                    expert_tile(group * GROUP + n // ET, n)
            for n in range(E // GROUP * GROUP * ET, E * ET):
                sp.wait_ge(s_wused, n - E_SLOTS + 1)
                expert_tile(n // ET, n)
            sp.wait_ge(s_wused, E * ET - E_SLOTS + 2)
            sp.dma_start(fing, final_g.rearrange("(a n) -> a n", a=1).partition_broadcast(P)[:, 0, :]).then_inc(s_fing, 16)
            for j in range(NT):
                sp.wait_ge(s_fin, j + 1)
                sp.dma_start(grid_tile(out, j), xs[:, j, :]).then_inc(s_out, 16)
            sp.wait_ge(s_out, 16 * NT)

        @block.gpsimd
        def _(pool):
            nc.gpsimd.memset(ones[:, :], 1.0).then_inc(s_ones, 1)
            nc.gpsimd.memset(nhalf[:, :], -0.5).then_inc(s_nhalf, 1)
            n_pow = [0]

            def power(a, n):
                n_pow[0] += 1
                pool.wait_ge(s_ss, n_pow[0])
                nc.gpsimd.tensor_tensor(a, a, nhalf[:, 0:n], ALU.pow).then_inc(s_rstd, 1)

            pool.wait_ge(s_nhalf, 1)
            for j in range(NT):
                power(stat[:, 8 + j:9 + j], 1)
            RW = na_rpb.shape[2]
            for m in range(4, NADA):
                if m == 10:
                    pool.wait_ge(s_red, 1)
                else:
                    pool.wait_ge(s_adaused, max(n for n in range(m) if ADA_MEM[n] == ADA_MEM[m]) + 1)
                pool.dma_start(ada_mem(m), ada_src(m)).then_inc(ada_sem(m), 16)
                if m == 5:
                    pool.wait_ge(s_pused, 1)
                if m == 6:
                    pool.wait_ge(s_adasb, 1)
                    pool.dma_start(adab, b_ada_rows(1)).then_inc(s_adab[1], 16)
                if 7 <= m <= 10:
                    pool.wait_ge(s_tdone, B_X + KD)
                    for cc in range(4 * (m - 7), 4 * (m - 7) + 4):
                        src = bass.AP(tensor=na_rpb.tensor, offset=15 - cc, ap=[[H * RW, ROWS], [RW, H * ROWS], [1, 32]])
                        pool.dma_start(braw[ROWS * cc:ROWS * cc + ROWS].rearrange("p r h c -> p (r h) c"),
                                       src).then_inc(s_rpb, 16)
                if m == 11:
                    pool.wait_ge(s_adasb, 2)
                    pool.dma_start(adab, b_ada_rows(2)).then_inc(s_adab[2], 16)
            pool.wait_ge(s_adaused, NADA)
            nc.gpsimd.memset(pb[:, :, 0:64], 0.0).then_inc(s_z, 1)
            nc.gpsimd.memset(pb[:, :, 320:384], 0.0).then_inc(s_z, 1)
            pool.wait_ge(s_adasb, 3)
            pool.wait_ge(s_biasr, 1)
            pool.wait_ge(s_const, 16)
            for d in range(16):
                j, k0, w, kb, nb, v = NAJ[d // 4]
                h = 2 * (d % 4)
                if d >= 2:
                    pool.wait_ge(s_sadd, d - 1)
                wv = 192 if v else 256
                c0 = 8 if v == 1 else 0
                for i in range(2):
                    last = nc.gpsimd.tensor_tensor(bm[:, d % 2, i, 0:wv],
                                            bias[:, h + i, c0:c0 + wv // 8, :].rearrange("p c r -> p (c r)"),
                                            mask[:, v, 0:wv], ALU.add)
                    last.then_inc(s_bm, 1)
                if v == 1:
                    nc.gpsimd.tensor_copy(bm[:, d % 2, :, 192:256],
                                          mask[:, 1, 192:256].unsqueeze(1).broadcast_to([P, 2, 64])).then_inc(s_bm, 1)
                if d - 1 in ROPE_AT:
                    n = 2 if ROPE_AT.index(d - 1) < NT else H
                    power(stat[:, 16:16 + n], n)
            for j in range(2 * NT):
                if j < 2:
                    pool.wait_ge(s_oread, j + 1)
                    nc.gpsimd.tensor_tensor(xs[:, j, :], xs[:, j, :], xh2[:, j, :], ALU.add).then_inc(s_opout, 1)
                power(stat[:, 8 + j % NT:9 + j % NT], 1)

        bm_count = lambda d: 2 * (d + 1) + max(0, d - 11)

        @block.scalar
        def _(act_):
            for i, v in enumerate((c, norm1_g, norm2_g)):
                act_.dma_start(vecs[8 * i:8 * i + 8, :], v.rearrange("b (k p) -> (b k) p", p=P)).then_inc(s_vec, 16)
            act_.dma_start(ident, consts[:, 0:P]).then_inc(s_ident, 16)
            act_.dma_start(adab, b_ada_rows(0)).then_inc(s_adab[0], 16)
            act_.wait_ge(s_vecT, 1)
            nc.scalar.activation(c32, ps[:, 7, 0:8].unsqueeze(2).broadcast_to([P, KD, 32]), ACT.Silu).then_inc(s_ct, 1)

            copy = lambda o, i: nc.scalar.activation(o, i, ACT.Copy)

            def out_batch(n, dst, view=lambda a: a):
                if n % 2:
                    act_.wait_ge(s_tdone, n + 1)
                    copy(dst, view(ps[:, 4 + n % 2, :])).then_inc(s_tout[1], 1)

            def hi(p):
                if p == 0:
                    act_.wait_ge(s_w0, 16)
                for m in tiles_of(p):
                    act_.wait_ge(s_w[f_slot(m)], 16 * uses_of(m))
                if p >= 2:
                    act_.wait_ge(s_pused, p - 1)
                for src, c0, n in piece(p):
                    last = copy(like(wh[:, p % 2, :], src, c0, n), src)
                last.then_inc(s_hi, 1)

            for k in range(KD):
                out_batch(B_X + k, hT[:, k, :])

            def h_hi(k):
                act_.wait_ge(s_h, k + 1)
                copy(hth[:, k, :], hT[:, k, :]).then_inc(s_thi, 1)

            hi(0)
            h_hi(0)
            h_hi(1)
            hi(1)
            for k in range(2, KD):
                h_hi(k)

            def proj_out(n):
                m, b = n // 4, n % 4
                if n < G_GATE and b < 3:
                    act_.wait_ge(s_proj, 3 * m + b + 1)
                elif n < G_GATE:
                    act_.wait_ge(s_pused, 4 * m + 4)
                else:
                    act_.wait_ge(s_pused, P_GATE + n - G_GATE + 1)
                src = ps[:, b if n < G_GATE else 7, :]
                if n < 4:
                    o = nc.scalar.activation(qk[:, n, :], src, ACT.Copy, scale=QS)
                elif n < 8:
                    o = copy(qk[:, n, :], src)
                elif n < G_QG:
                    if b == 0:
                        act_.wait_ge(s_colps, 1)
                    o = copy(vy[:, b, :], src)
                elif n < G_KV:
                    if b == 0:
                        act_.wait_ge(s_biasr, 1)
                    o = copy(qy[:, 0, b, :].rearrange("p (i g d) -> p g i d", g=2, i=4),
                             src.rearrange("p (g i d) -> p g i d", g=2, i=4))
                elif n < G_GATE:
                    if b == 0:
                        act_.wait_ge(s_adaused, NADA)
                    o = copy(kvg[:, b, :], src[:, 0:256])
                elif n < G_GATE + KD:
                    o = copy(sig[:, n - G_GATE, :], src)
                else:
                    o = copy(sigb[:, n - G_GATE - KD, :], src)
                o.then_inc(s_projout, 1)

            def exps(d):
                for i in range(2):
                    u = 2 * d + i
                    act_.wait_ge(s_nmax, d + 1)
                    if u >= 4:
                        act_.wait_ge(s_tdone, pt_batch(d - 2, i) + 1)
                    else:
                        act_.wait_ge(s_z, 2)
                    if d < 16:
                        j, k0, w, kb, nb, v = NAJ[d // 4]
                        o, s = pb[:, u % 4, k0 - kb:k0 - kb + w], ssb[:, i, 0:w]
                    else:
                        o, s = pb[:, u % 4, :], ps[:, 2 * (d % 2) + i, :]
                    nc.scalar.activation(o, s, ACT.Exp, bias=nmax[:, u:u + 1],
                                         accum_out=rsum[:, u:u + 1]).then_inc(s_p, 1)

            def pt_out(d):
                for i in range(2):
                    n = pt_batch(d, i)
                    if n % 2:
                        act_.wait_ge(s_tdone, n + 1)
                        if d:
                            act_.wait_ge(s_av, d)
                        w = P * NAJ[d // 4][4] if d < 16 else T
                        copy(ptb[:, i, 0:w], ps[:, 4 + n % 2, 0:w]).then_inc(s_tout[1], 1)

            act_.dma_start(cst[:, P:], consts[:, P:]).then_inc(s_const, 16)
            act_.dma_start(gains[:, 0, :], q_norm_g.partition_broadcast(P)[:, 0, :]).then_inc(s_small, 16)
            act_.dma_start(gains[:, 1, :], k_norm_g.partition_broadcast(P)[:, 0, :]).then_inc(s_small, 16)
            act_.dma_start(wr[:, :, :], w_router.rearrange("(k p) e -> p k e", p=P)).then_inc(s_small, 16)
            for p in range(1, P_GATE):
                hi(p + 1)
                if p % 4 == 3:
                    for b in range(4):
                        proj_out(p - 3 + b)
            for d in range(18):
                if d >= 2:
                    pt_out(d - 2)
                if d < 16:
                    exps(d)
                if d % 2 == 0:
                    hi(P_GATE + d // 2 + 1)
                if d == 17:
                    out_batch(B_K, kt)
                    for j in range(NT):
                        out_batch(B_Q + j, qt[:, :, P * j:P * j + P], lambda a: a.rearrange("p (b t) -> p b t", b=4))
                if d % 2:
                    proj_out(G_GATE + d // 2)

            def y_hi(i):
                act_.wait_ge(s_tout[0], (B_GQ + 1) // 2)
                act_.wait_ge(s_tout[1], B_GQ // 2)
                act_.wait_ge(s_pused, P_BR)
                copy(hth[:, i, :], ytn[:, i, :]).then_inc(s_thi, 1)

            def yg_hi(j):
                n = yg_batch(j)
                act_.wait_ge(s_tdone, n + 1)
                copy(hth[:, 4:8, P * j:P * j + P], ps[:, 4 + n % 2, :].rearrange("p (i t) -> p i t", i=4)).then_inc(s_thi, 1)

            for d in range(16, 34):
                if d >= 18:
                    pt_out(d - 2)
                for j in {32: (0,), 33: (1, 2)}.get(d, ()):
                    yg_hi(j)
                if d < 32:
                    exps(d)
                if d == 17:
                    for i in range(4):
                        out_batch(B_YN + i, ytn[:, i, :])
                if d % 2 == 0 and d <= 30:
                    hi(P_GATE + (d + 2) // 2 + 1)
                if d % 2 and d < 30:
                    proj_out(G_GATE + (d + 2) // 2)
                if d in (30, 31):
                    y_hi(2 * (d - 30))
                    y_hi(2 * (d - 30) + 1)
            yg_hi(3)
            act_.wait_ge(s_projout, N_PROJ)
            def merged_hi(k):
                act_.wait_ge(s_pused, P_OUT)
                act_.wait_ge(s_brout, k + 1)
                copy(hth[:, k, :], sig[:, k, :]).then_inc(s_thi, 1)

            for b in range(KD):
                for g in (sig, sigb):
                    nc.scalar.activation(g[:, b, :], g[:, b, :], ACT.Sigmoid).then_inc(s_sg, 1)
                if b == KD - 1:
                    merged_hi(0)
                    merged_hi(1)
                hi(P_BR + 2 + b)
            for k in range(2, KD):
                merged_hi(k)
                if k in (3, 5, 7):
                    hi(P_OUT + 2 + (k - 3) // 2)

            def square(j):
                act_.wait_ge(s_opout, j + 1)
                nc.scalar.activation(xh2[:, j, :], xs[:, j, :], ACT.Square, scale=D ** -0.5,
                                     accum_out=stat[:, j:j + 1]).then_inc(s_sq, 1)

            def h2_out(j):
                for i in range(2):
                    n = B_X2 + 2 * j + i
                    if n % 2:
                        act_.wait_ge(s_tdone, n + 1)
                        for k in range(4 * i, 4 * i + 4):
                            last = nc.scalar.activation(h2t[:, k, P * j:P * j + P], ps[:, 4 + n % 2, P * (k % 4):P * (k % 4) + P],
                                                        ACT.Identity, bias=s2[:, k:k + 1], scale=a2[:, k:k + 1])
                        last.then_inc(s_tout[1], 1)

            for p in range(P_OUT + 5, N_PIECE):
                hi(p)
                if p in (P_OUT + 11, P_OUT + 12):
                    square(p - P_OUT - 11)
                if p == P_OUT + 15:
                    h2_out(0)
            square(2)
            h2_out(1)
            square(3)
            for j in (2, 3):
                h2_out(j)
            act_.wait_ge(s_nm2, 1)
            nc.scalar.activation(aff[:, :, :], aff[:, :, :], ACT.Exp).then_inc(s_ex, 1)
            if B_AFF % 2:
                act_.wait_ge(s_tdone, B_AFF + 1)
                copy(work.rearrange("e (r c) -> e r c", c=COLS),
                     ps[0:E, 4 + B_AFF % 2, :].rearrange("e (c r) -> e r c", r=ROWS)).then_inc(s_tout[1], 1)
            if B_SLOT % 2:
                act_.wait_ge(s_tdone, B_SLOT + 1)
                copy(slots[:, :, 0:E], ps[:, 4 + B_SLOT % 2, 0:NT * E].rearrange("p (j e) -> p j e", j=NT)).then_inc(s_tout[1], 1)

            with act_.Fori(0, E) as e:
                act_.wait_ge(s_xt, e + 1)
                for k in range(KD):
                    c0 = P * (k % 4) + CAP * (k // 4)
                    nc.scalar.activation(xinT[:, k, :], ps[:, 5, c0:c0 + CAP], ACT.Identity, bias=s2[:, k:k + 1],
                                         scale=a2[:, k:k + 1]).then_inc(s_xinT, 1)
                for g in range(2):
                    act_.wait_ge(s_wused, e * ET + (8 * g + 4))
                    nc.scalar.activation(silu[:, g, :], ps[:, 2 * g, :], ACT.Silu).then_inc(s_silu, 1)
            for j in range(NT):
                act_.wait_ge(s_cbout, NT * (E - 1) + j + 2)
                square(j)

        @block.vector
        def _(dve):
            chain = [0]

            def link(ins):
                chain[0] += 1
                ins.then_inc(s_dve, 1)
                dve.wait_ge(s_dve, chain[0])

            n_pow = [0]

            def mean_square(j, scratch):
                link(nc.vector.tensor_tensor_reduce(out=scratch[:, j, :], in0=xs[:, j, :], in1=xs[:, j, :], scale=1.0 / D,
                                                    scalar=0.0, op0=ALU.mult, op1=ALU.add, accum_out=stat[:, j:j + 1]))
                nc.vector.tensor_scalar(stat[:, 8 + j:9 + j], stat[:, j:j + 1], EPS, None, ALU.add).then_inc(s_ss, 1)

            def rstd_in():
                n_pow[0] += 1
                dve.wait_ge(s_rstd, n_pow[0])

            def normalise(j, dst, ready):
                rstd_in()
                nc.vector.tensor_scalar(dst[:, j, :], xs[:, j, :], stat[:, 8 + j:9 + j], None, ALU.mult).then_inc(ready, 1)

            for j in range(NT):
                dve.wait_ge(s_x[j], 16)
                mean_square(j, xh)
            for j in range(NT):
                normalise(j, xh, s_xh)
            dve.wait_ge(s_ct, 1)
            nc.vector.tensor_copy(col[:, 0:2, :], ps[:, 7, 8:24].rearrange("p (v k) -> p v k", v=2))

            def out_batch(n, dst, view=lambda a: a):
                if n % 2 == 0:
                    dve.wait_ge(s_tdone, n + 1)
                    nc.vector.tensor_copy(dst, view(ps[:, 4 + n % 2, :])).then_inc(s_tout[0], 1)

            for k in range(KD):
                out_batch(B_X + k, hT[:, k, :])

            raw = lambda a: a.bitcast(f32)

            def lo(p):
                dve.wait_ge(s_hi, p + 1)
                for src, c0, n in piece(p):
                    last = nc.vector.tensor_tensor(like(wl[:, p % 2, :], src, c0, n), src,
                                                   raw(like(wh[:, p % 2, :], src, c0, n)), ALU.subtract)
                last.then_inc(s_lo, 1)

            n_thi = [0]

            def t_lo(k, src, ready):
                n_thi[0] += 1
                dve.wait_ge(s_thi, n_thi[0])
                nc.vector.tensor_tensor(htl[:, k, :], src, raw(hth[:, k, :]), ALU.subtract).then_inc(ready, 1)

            def yg_lo(j):
                n, t = yg_batch(j), slice(P * j, P * j + P)
                n_thi[0] += 1
                dve.wait_ge(s_thi, n_thi[0])
                nc.vector.tensor_tensor(htl[:, 4:8, t], ps[:, 4 + n % 2, :].rearrange("p (i t) -> p i t", i=4),
                                        raw(hth[:, 4:8, t]), ALU.subtract).then_inc(s_tout[n % 2], 1)

            def ada_rows(g):
                if g:
                    dve.wait_ge(s_red, g)
                else:
                    dve.wait_ge(s_adaused, 4)
                dve.wait_ge(s_adab[g], 16)
                parts = ([(adar[0], 0, P)], [(grow[0:64, :], 0, 64), (adar[1][64:P], 64, P)],
                         [(adar[1][0:64], 0, 64), (grow[64:P, :], 64, P)])[g]
                for dst, p0, p1 in parts:
                    last = nc.vector.tensor_tensor(dst, ps[p0:p1, 6, :], adab[p0:p1, :], ALU.add)
                last.then_inc(s_adasb, 1)

            def modulation(n, shift, scale, s, a, gain):
                dve.wait_ge(s_colps, n)
                rows = ps[:, 7, :].rearrange("p (b i r) -> p i b r", b=4, i=4)[:, :, :, 0]
                two = lambda v: v.rearrange("p (i b) -> p i b", i=2)
                link(nc.vector.tensor_copy(two(s), rows[:, shift:shift + 2, :]))
                nc.vector.scalar_tensor_tensor(out=two(a), in0=rows[:, scale:scale + 2, :], scalar=1.0,
                                               in1=two(gain), op0=ALU.add, op1=ALU.mult).then_inc(s_cols, 1)
                dve.wait_ge(s_cols, n)

            def ada_step(t):
                m, kk = 4 + t // 2, t % 2
                k, total, rows = 2 * (m % 4) + kk, ada_sum(m // 4), ada_mem(m)[:, kk, :]
                if kk == 0:
                    dve.wait_ge(ada_sem(m), ada_count(m))
                if k == 0:
                    step = nc.vector.tensor_scalar(total, rows, c32[:, k, 0:1], None, ALU.mult)
                else:
                    step = nc.vector.scalar_tensor_tensor(out=total, in0=rows, scalar=c32[:, k, 0:1], in1=total,
                                                          op0=ALU.mult, op1=ALU.add)
                if kk == 0:
                    link(step)
                else:
                    step.then_inc(s_adaused, 1)
                    dve.wait_ge(s_adaused, m + 1)

            ada_rows(0)
            lo(0)
            modulation(1, 0, 2, s1, a1, n1c)
            dve.wait_ge(s_tout[1], KD // 2)

            def modulate(k):
                nc.vector.tensor_scalar(hT[:, k, :], hT[:, k, :], a1[:, k:k + 1], s1[:, k:k + 1], ALU.mult,
                                        ALU.add).then_inc(s_h, 1)

            modulate(0)
            modulate(1)
            for k in range(KD):
                t_lo(k, hT[:, k, :], s_ht)
                if k + 2 < KD:
                    modulate(k + 2)
                if k == 1:
                    lo(1)
            for p in range(2, P_GATE + 1):
                lo(p)
                if p == 7:
                    dve.wait_ge(s_small, 48)
                    nc.vector.tensor_scalar(gains[:, 1, :], gains[:, 1, :], HD ** 0.5, None, ALU.mult).then_inc(s_gain, 1)
                if p == 14:
                    dve.wait_ge(s_rpb, 16 * 16)
                    nc.vector.tensor_copy(bias[:, :, :, :].rearrange("p h c r -> p r h c"),
                                          braw[:, ::-1, :, :]).then_inc(s_biasr, 1)
                if p <= 17:
                    ada_step(p - 2)
                if p == 11:
                    ada_rows(1)
                if p == 20:
                    ada_rows(2)
                    modulation(2, 2, 0, s2, a2, n2c)

            def rope_of(r):
                j, nh = r % NT, 2 if r < NT else H
                src = (kvg[:, j, 0:P] if r < NT else qy[:, 0, j, :]).rearrange("p (h d) -> p h d", h=nh)
                return j, nh, src, rt[:, 0:nh * HD].rearrange("p (h d) -> p h d", h=nh), stat[:, 16:16 + nh]

            def rope_squares(r):
                j, nh, src, tmp, st = rope_of(r)
                link(nc.vector.tensor_tensor(tmp, src, src, ALU.mult))
                link(nc.vector.tensor_reduce(out=st, in_=tmp, axis=X, op=ALU.add))
                nc.vector.tensor_scalar(st, st, HD * EPS, None, ALU.add).then_inc(s_ss, 1)

            def rope_scale(r):
                j, nh, src, tmp, st = rope_of(r)
                gain = gains[:, 1 if r < NT else 0, :]
                rstd_in()
                link(nc.vector.tensor_tensor(tmp, src, st.unsqueeze(2).broadcast_to([P, nh, HD]), ALU.mult))
                link(nc.vector.tensor_tensor(tmp, tmp, gain.unsqueeze(1).broadcast_to([P, nh, HD]), ALU.mult))

            def rope_rotate(r):
                j, nh, src, tmp, st = rope_of(r)
                t2 = rt[:, 512:512 + nh * HD // 2].rearrange("p (h d) -> p h d", h=nh)
                t3 = rt[:, 768:768 + nh * HD // 2].rearrange("p (h d) -> p h d", h=nh)
                even, odd = tmp[:, :, 0:HD:2], tmp[:, :, 1:HD:2]
                cj = cos[:, j, :].unsqueeze(1).broadcast_to([P, nh, HD // 2])
                sj = sin[:, j, :].unsqueeze(1).broadcast_to([P, nh, HD // 2])
                nc.vector.tensor_tensor(t2, even, cj, ALU.mult)
                link(nc.vector.tensor_tensor(t3, odd, sj, ALU.mult))
                link(nc.vector.tensor_tensor(src[:, :, 0:HD:2], t2, t3, ALU.subtract))
                nc.vector.tensor_tensor(t2, even, sj, ALU.mult)
                link(nc.vector.tensor_tensor(t3, odd, cj, ALU.mult))
                nc.vector.tensor_tensor(src[:, :, 1:HD:2], t2, t3, ALU.add).then_inc(s_rope, 1)

            def softmax(d):
                if d < 16:
                    j, k0, w, kb, nb, v = NAJ[d // 4]
                    dve.wait_ge(s_s, 2 * d + 2)
                    dve.wait_ge(s_bm, bm_count(d))
                    if d:
                        dve.wait_ge(s_p, 2 * d)
                    nc.vector.tensor_tensor(ssb[:, :, 0:w], ps[:, 2 * (d % 2):2 * (d % 2) + 2, 0:w],
                                            bm[:, d % 2, :, 0:w], ALU.add).then_inc(s_sadd, 1)
                    dve.wait_ge(s_sadd, d + 1)
                    src = ssb[:, :, 0:w]
                else:
                    dve.wait_ge(s_s, 2 * d + 2)
                    src = ps[:, 2 * (d % 2):2 * (d % 2) + 2, :]
                nc.vector.tensor_reduce(out=nmax[:, 2 * d:2 * d + 2], in_=src, axis=X, op=ALU.max,
                                        negate=True).then_inc(s_nmax, 1)

            def pt_out(d):
                for i in range(2):
                    n = pt_batch(d, i)
                    if n % 2 == 0:
                        dve.wait_ge(s_tdone, n + 1)
                        if d:
                            dve.wait_ge(s_av, d)
                        w = P * NAJ[d // 4][4] if d < 16 else T
                        nc.vector.tensor_copy(ptb[:, i, 0:w], ps[:, 4, 0:w]).then_inc(s_tout[0], 1)

            def y_out(d):
                dve.wait_ge(s_p, 2 * d + 2)
                link(nc.vector.reciprocal(rinv[:, 2 * d:2 * d + 2], rsum[:, 2 * d:2 * d + 2]))
                dve.wait_ge(s_av, d + 1)
                if d < 16:
                    j, h, step = NAJ[d // 4][0], 2 * (d % 4), 1
                else:
                    j, h, step = (d - 16) // 4, d % 4, 4
                    if d == 16:
                        dve.wait_ge(s_tdone, B_YN + 4)
                dst = ytok[:, j, :].rearrange("p (h d) -> p h d", h=H)[:, h:h + step + 1:step, :]
                nc.vector.tensor_tensor(dst, ps[:, 6, 0:P].rearrange("p (h d) -> p h d", h=2),
                                        rinv[:, 2 * d:2 * d + 2].unsqueeze(2).broadcast_to([P, 2, HD]),
                                        ALU.mult).then_inc(s_y, 1)

            dve.wait_ge(s_gain, 1)
            dve.wait_ge(s_projout, G_GATE)
            for d in range(18):
                if d >= 2:
                    pt_out(d - 2)
                if d < 16:
                    softmax(d)
                if d == 17:
                    out_batch(B_K, kt)
                    for j in range(NT):
                        out_batch(B_Q + j, qt[:, :, P * j:P * j + P], lambda a: a.rearrange("p (b t) -> p b t", b=4))
                if d in SCALE_AT:
                    rope_scale(SCALE_AT.index(d))
                if d in ROTATE_AT:
                    rope_rotate(ROTATE_AT.index(d))
                if d in ROPE_AT:
                    rope_squares(ROPE_AT.index(d))
                if d % 2 == 0:
                    lo(P_GATE + d // 2 + 1)
                if d >= 2:
                    y_out(d - 2)
            for d in range(16, 34):
                if d >= 18:
                    pt_out(d - 2)
                for j in {32: (0,), 33: (1, 2)}.get(d, ()):
                    yg_lo(j)
                if d < 32:
                    softmax(d)
                if d == 17:
                    for i in range(4):
                        out_batch(B_YN + i, ytn[:, i, :])
                if d % 2 == 0 and d <= 30:
                    lo(P_GATE + (d + 2) // 2 + 1)
                if 30 <= d <= 32:
                    dve.wait_ge(s_bcps, d - 29)
                    dst = (gate2, gate1[:, 0:512], gate1[:, 512:D])[d - 30]
                    nc.vector.tensor_copy(dst, ps[:, 7, :]).then_inc(s_bc, 1)
                if d >= 18:
                    y_out(d - 2)
                if d == 31:
                    for i in range(4):
                        t_lo(i, ytn[:, i, :], s_ht)
            yg_lo(3)
            for b in range(KD):
                q = 2 * (b % 2)
                dve.wait_ge(s_sg, 2 * b + 2)
                dve.wait_ge(s_pused, P_BR + b + 1)
                nc.vector.tensor_tensor(sig[:, b, :], sig[:, b, :], ps[:, q, :], ALU.mult)
                nc.vector.tensor_tensor(sigb[:, b, :], sigb[:, b, :], ps[:, q + 1, :], ALU.mult).then_inc(s_bread, 1)
                if b == KD - 1:
                    t_lo(0, sig[:, 0, :], s_ht)
                dve.wait_ge(s_bread, b + 1)
                nc.vector.tensor_tensor(sig[:, b, :], sig[:, b, :], sigb[:, b, :], ALU.add).then_inc(s_brout, 1)
                if b == KD - 1:
                    t_lo(1, sig[:, 1, :], s_ht)
                lo(P_BR + 2 + b)
            for k in range(2, KD):
                t_lo(k, sig[:, k, :], s_ht)
                if k in (3, 5, 7):
                    lo(P_OUT + 2 + (k - 3) // 2)

            def gated(j):
                q = (0, 2, 6, 0)[j]
                if j % 2 == 0:
                    dve.wait_ge(s_op, j // 2 + 1)
                else:
                    dve.wait_ge(s_pused, P_OUT + KD * (j // 2 + 1))
                nc.vector.tensor_tensor(xh2[:, j, :], ps[:, q:q + 2, :].rearrange("p a n -> p (a n)"), gate1,
                                        ALU.mult).then_inc(s_oread, 1)

            def residual(j):
                dve.wait_ge(s_oread, j + 1)
                nc.vector.tensor_tensor(xs[:, j, :], xs[:, j, :], xh2[:, j, :], ALU.add).then_inc(s_opout, 1)

            def add_eps(n):
                j = n % NT
                dve.wait_ge(s_sq, n + 1)
                nc.vector.tensor_scalar(stat[:, 8 + j:9 + j], stat[:, j:j + 1], EPS, None, ALU.add).then_inc(s_ss, 1)

            def h2_out(j):
                for i in range(2):
                    n = B_X2 + 2 * j + i
                    if n % 2 == 0:
                        dve.wait_ge(s_tdone, n + 1)
                        for k in range(4 * i, 4 * i + 4):
                            last = nc.vector.tensor_scalar(h2t[:, k, P * j:P * j + P], ps[:, 4 + n % 2, P * (k % 4):P * (k % 4) + P],
                                                           a2[:, k:k + 1], s2[:, k:k + 1], ALU.mult, ALU.add)
                        last.then_inc(s_tout[0], 1)

            after = {8: lambda: gated(0), 9: lambda: gated(1), 11: lambda: add_eps(0),
                     12: lambda: normalise(0, xh2, s_xh2), 13: lambda: (add_eps(1), normalise(1, xh2, s_xh2)),
                     15: lambda: h2_out(0)}
            for p in range(P_OUT + 5, N_PIECE):
                lo(p)
                if p - P_OUT in after:
                    after[p - P_OUT]()
            for j in (2, 3):
                gated(j)
                residual(j)
            add_eps(2)
            h2_out(1)
            normalise(2, xh2, s_xh2)
            add_eps(3)
            normalise(3, xh2, s_xh2)
            for j in (2, 3):
                h2_out(j)
            dve.wait_ge(s_log, 1)
            lg = ps[:, 3, 0:NT * E].rearrange("p (j e) -> p j e", j=NT)
            bce = lambda a: a.unsqueeze(2).broadcast_to([P, NT, E])
            link(nc.vector.tensor_reduce(out=stat[:, 48:52], in_=lg, axis=X, op=ALU.max))
            nc.vector.tensor_tensor(aff[:, :, :], lg, bce(stat[:, 48:52]), ALU.subtract).then_inc(s_nm2, 1)
            dve.wait_ge(s_ex, 1)
            link(nc.vector.tensor_reduce(out=stat[:, 52:56], in_=aff[:, :, :], axis=X, op=ALU.add))
            link(nc.vector.reciprocal(stat[:, 56:60], stat[:, 52:56]))
            nc.vector.tensor_tensor(aff[:, :, :], aff[:, :, :], bce(stat[:, 56:60]), ALU.mult).then_inc(s_aff, 1)
            nc.vector.memset(onesr, 1.0)
            nc.vector.memset(slots[:, :, E:E + 1], 0.0).then_inc(s_cbout, 1)
            if B_AFF % 2 == 0:
                dve.wait_ge(s_tdone, B_AFF + 1)
                link(nc.vector.tensor_copy(work.rearrange("e (r c) -> e r c", c=COLS),
                                           ps[0:E, 4, :].rearrange("e (c r) -> e r c", r=ROWS)))
            else:
                dve.wait_ge(s_tout[1], B_AFF // 2 + 1)
            for r in range(CAP // 8):
                link(nc.vector.max(out=top8[:, 8 * r:8 * r + 8], in_=work))
                link(nc.vector.match_replace(out=work, in_to_replace=top8[:, 8 * r:8 * r + 8], in_values=work,
                                             imm_value=-1.0))
            link(nc.vector.tensor_scalar(sel, work, 0.0, None, ALU.is_lt))
            link(nc.vector.tensor_tensor_scan(out=cum, data0=onesr, data1=sel, initial=0.0, op0=ALU.mult, op1=ALU.add))
            nc.vector.tensor_tensor(slot_e.rearrange("e (c r) -> e r c", r=ROWS), cum.rearrange("e (r c) -> e r c", c=COLS),
                                    sel.rearrange("e (r c) -> e r c", c=COLS), ALU.mult).then_inc(s_slot, 1)
            if B_SLOT % 2 == 0:
                dve.wait_ge(s_tdone, B_SLOT + 1)
                nc.vector.tensor_copy(slots[:, :, 0:E], ps[:, 4, 0:NT * E].rearrange("p (j e) -> p j e", j=NT)).then_inc(s_tout[0], 1)
                dve.wait_ge(s_tout[0], B_SLOT // 2 + 1)
            else:
                dve.wait_ge(s_tout[1], B_SLOT // 2 + 1)

            def one_hots(e, waits=True):
                for j in range(NT):
                    last = nc.vector.tensor_scalar(pick[:, j, :], iota[:, 0:CAP], slots[:, j, bass.ds(e, 1)], None,
                                                   ALU.is_equal)
                last.then_inc(s_pick, 1)
                for j in range(NT):
                    last = nc.vector.tensor_scalar(give[:, j, :], iota, slots[:, j, bass.ds(e, 1)], aff[:, j, bass.ds(e, 1)],
                                                   ALU.is_equal, ALU.mult)
                last.then_inc(s_gready, 1)

            one_hots(0)

            def expert(e, more):
                dve.wait_ge(s_gath, e + 1)
                nc.vector.tensor_copy(xin, ps[:, 7, :]).then_inc(s_xin, 1)
                dve.wait_ge(s_give, e + 1)
                nc.vector.tensor_copy(giveT, ps[:, 6, :]).then_inc(s_giveT, 1)
                if more:
                    one_hots(e + 1)
                for g in range(2):
                    dve.wait_ge(s_silu, 2 * e + g + 1)
                    dve.wait_ge(s_wused, e * ET + (8 * g + 8))
                    nc.vector.tensor_tensor(act[:, g, :], silu[:, g, :], ps[:, 2 * g + 1, :], ALU.mult).then_inc(s_act, 1)
                for g in range(2):
                    dve.wait_ge(s_at, 2 * e + g + 1)
                    dst = actT[:, 8 * g:8 * g + 8, :].rearrange("p (h b) s -> p b h s", h=2)
                    nc.vector.tensor_copy(dst, ps[:, 5 + g, :].rearrange("p (b h s) -> p b h s", b=4, h=2)).then_inc(s_actT, 1)
                dve.wait_ge(s_wused, e * ET + ET)
                nc.vector.tensor_tensor(ysb, ps[:, 4, :], gate2, ALU.mult).then_inc(s_ysb, 1)

            def add_share(e, j):
                q = 2 * (j % 2)
                dve.wait_ge(s_cb, 4 * e + j + 1)
                nc.vector.tensor_tensor(xs[:, j, :], xs[:, j, :], ps[:, q:q + 2, :].rearrange("p a n -> p (a n)"),
                                        ALU.add).then_inc(s_cbout, 1)

            with dve.Fori(0, E - 1) as e:
                expert(e, True)
                for j in range(NT):
                    add_share(e, j)
            expert(E - 1, False)

            def final(j):
                rstd_in()
                nc.vector.scalar_tensor_tensor(out=xs[:, j, :], in0=xs[:, j, :], scalar=stat[:, 8 + j:9 + j], in1=fing,
                                               op0=ALU.mult, op1=ALU.mult).then_inc(s_fin, 1)

            dve.wait_ge(s_fing, 16)
            for j in range(NT):
                add_share(E - 1, j)
                if j:
                    add_eps(NT + j - 1)
                if j >= 2:
                    final(j - 2)
            add_eps(2 * NT - 1)
            for j in (2, 3):
                final(j)

        @block.tensor
        def _(pe):
            mm = nc.tensor.matmul

            def split_mm(out, left, right, start, stop):
                (lh, ll), (rh, rl) = left, right
                mm(out, lh, rh, start=start, stop=False)
                mm(out, lh, rl, start=False, stop=False)
                return mm(out, ll, rh, start=False, stop=stop)

            def weights(p, k):
                return [a[:, p % 2, 0:512 if P_KV <= p < P_GATE else 1024].rearrange("p (k n) -> p k n", k=k) for a in (wh, wl)]

            acts = lambda k, c0=0, c1=T: (hth[:, k, c0:c1], htl[:, k, c0:c1])
            cut = lambda w, k, c0, c1: (w[0][:, k, c0:c1], w[1][:, k, c0:c1])

            pe.wait_ge(s_vec, 48)
            pe.wait_ge(s_ident, 16)
            nc.tensor.transpose(ps[:, 7, 0:24], vecs[:, :], ident[0:24, 0:24]).then_inc(s_vecT, 1)

            def bank_free(n):
                if n >= 2:
                    pe.wait_ge(s_tout[n % 2], n // 2)

            def batches_out(n):
                pe.wait_ge(s_tout[0], (n + 1) // 2)
                pe.wait_ge(s_tout[1], n // 2)

            def batch(n, src, parts=NT):
                bank_free(n)
                for i in range(parts):
                    last = nc.tensor.transpose(ps[:, 4 + n % 2, P * i:P * i + P], src(i), ident)
                last.then_inc(s_tdone, 1)

            def ada(m):
                pe.wait_ge(ada_sem(m), ada_count(m))
                for kk in range(2):
                    if (m, kk) == (3, 1):
                        pe.wait_ge(s_ada[7], 16)
                    k = 2 * m + kk
                    for i in range(4):
                        last = mm(ps[32 * i:32 * i + 32, 6, :], c32[:, k, :], ada_mem(m)[:, kk, 512 * i:512 * i + 512],
                                  start=(k == 0), stop=(k == KD - 1), skip_group_check=True)
                last.then_inc(s_adaused, 1)

            def ada_reduce(g):
                pe.wait_ge(s_adaused, 4 * g + 4)
                pe.wait_ge(s_adasb, g)
                for i in range(4):
                    last = mm(ps[32 * i:32 * i + 32, 6, :], ones[:, 0:32], ada_sum(g)[:, 512 * i:512 * i + 512], start=True,
                              stop=True)
                last.then_inc(s_red, 1)

            def columns(v):
                for b in range(4):
                    last = nc.tensor.transpose(ps[:, 7, P * b:P * b + P], adar[v][:, P * b:P * b + P], ident)
                last.then_inc(s_colps, 1)

            def keep_clock(n, bank, moving):
                for _ in range(n):
                    mm(ps[:, bank, :], ident, moving, start=True, stop=True)

            pe.wait_ge(s_ct, 1)
            pe.wait_ge(s_ones, 1)
            ada(0)
            pe.wait_ge(s_xh, NT)
            for k in range(KD):
                batch(B_X + k, lambda j: xh[:, j, P * k:P * k + P])
                if k == 3:
                    ada(1)
            ada(2)
            keep_clock(2, 2, xs[:, 0, 0:512])
            ada(3)
            pe.wait_ge(s_adasb, 1)
            columns(0)
            keep_clock(2, 2, xs[:, 0, 0:512])

            for p in range(P_GATE):
                m, q = p // 4, p % 4
                pe.wait_ge(s_lo, p + 1)
                w = weights(p, 2)
                width = 256 if m == T_KV else 512
                for b, kk in ([(b, kk) for b in range(4) for kk in range(2)] if p else
                              [(b, kk) for kk in range(2) for b in range(4)]):
                    k = 2 * q + kk
                    if m == 0 and b == 0:
                        pe.wait_ge(s_ht, k + 1)
                    if m and q == 0 and kk == 0:
                        pe.wait_ge(s_projout, 4 * m - 3 + b)
                    if m < 2:
                        left, right = cut(w, kk, P * b, P * b + P), acts(k)
                    else:
                        left, right = acts(k, P * b, P * b + P), cut(w, kk, 0, width)
                    last = split_mm(ps[:, b, 0:width], left, right, k == 0, k == KD - 1)
                    if q == 3 and kk and b < 3:
                        last.then_inc(s_proj, 1)
                last.then_inc(s_pused, 1)
                if p in (9, 18):
                    ada_reduce(1 if p == 9 else 2)
                if p == 19:
                    pe.wait_ge(s_adasb, 3)
                    pe.wait_ge(s_cols, 1)
                    columns(1)

            def gates(g, half):
                p = P_GATE + g
                if half == 0:
                    pe.wait_ge(s_lo, p + 1)
                    pe.wait_ge(s_projout, G_GATE + g)
                w = weights(p, KD)
                for k in range(4 * half, 4 * half + 4):
                    last = split_mm(ps[:, 7, :], cut(w, k, 0, P), acts(k), k == 0, k == KD - 1)
                if half:
                    last.then_inc(s_pused, 1)

            def scores(d):
                if d >= 18:
                    pe.wait_ge(s_p, 2 * d - 2)
                elif d >= 2:
                    pe.wait_ge(s_sadd, d - 1)
                for i in range(2):
                    r = slice(HD * i, HD * i + HD)
                    if d < 16:
                        j, k0, w, kb, nb, v = NAJ[d // 4]
                        q, k = qk[r, d % 4, P * j:P * j + P], qk[r, 4 + d % 4, k0:k0 + w]
                    else:
                        j, w = (d - 16) // 4, T
                        q, k = qt[r, d % 4, P * j:P * j + P], kt[r, :]
                    mm(ps[:, 2 * (d % 2) + i, 0:w], q, k, start=True, stop=True).then_inc(s_s, 1)

            def transposes(d):
                for i in range(2):
                    u = 2 * d + i
                    n = pt_batch(d, i)
                    pe.wait_ge(s_p, u + 1)
                    bank_free(n)
                    nb = NAJ[d // 4][4] if d < 16 else NT
                    for b in range(nb):
                        last = nc.tensor.transpose(ps[:, 4 + n % 2, P * b:P * b + P], pb[:, u % 4, P * b:P * b + P], ident)
                    last.then_inc(s_tdone, 1)

            def weighted(d):
                batches_out(pt_batch(d, 1) + 1)
                if d:
                    pe.wait_ge(s_y, d)
                for i in range(2):
                    nb = NAJ[d // 4][4] if d < 16 else NT
                    for b in range(nb):
                        if d < 16:
                            v = vy[:, NAJ[d // 4][3] // P + b, HD * (2 * (d % 4) + i):HD * (2 * (d % 4) + i) + HD]
                        else:
                            v = kvg[:, b, P + HD * i:P + HD * i + HD]
                        last = mm(ps[:, 6, HD * i:HD * i + HD], ptb[:, i, P * b:P * b + P], v, start=(b == 0),
                                  stop=(b == nb - 1))
                last.then_inc(s_av, 1)

            def gate_rows(i):
                if i == 0:
                    pe.wait_ge(s_projout, N_PROJ)
                else:
                    pe.wait_ge(s_bc, i)
                keep_clock(1, 7, xs[:, 0, 0:512])
                if i == 0:
                    for h in range(2):
                        q = 64 + 32 * h
                        last = mm(ps[64 * h:64 * h + 64, 7, :], ones[q:q + 1, 0:64], grow[q:q + 1, :], start=True, stop=True)
                    last.then_inc(s_bcps, 1)
                elif i < 3:
                    q = 32 * (i - 1)
                    mm(ps[:, 7, :], ones[q:q + 1, :], grow[q:q + 1, :], start=True, stop=True).then_inc(s_bcps, 1)

            pe.wait_ge(s_projout, G_GATE)
            pe.wait_ge(s_cols, 2)
            for d in range(18):
                if d < 16:
                    scores(d)
                if d == 17:
                    pe.wait_ge(s_rope, 8)
                    batch(B_K, lambda j: kvg[:, j, 0:P])
                    for j in range(NT):
                        batch(B_Q + j, lambda b: qy[:, 0, j, P * b:P * b + P])
                gates(d // 2, d % 2)
                if d >= 2:
                    weighted(d - 2)
                if 1 <= d <= 16:
                    transposes(d - 1)
            batches_out(B_YN)
            for d in range(16, 34):
                if d < 32:
                    scores(d)
                if d < 30:
                    gates((d + 2) // 2, d % 2)
                else:
                    gate_rows(d - 30)
                if d == 17:
                    pe.wait_ge(s_y, 16)
                    for i in range(4):
                        batch(B_YN + i, lambda j: ytok[:, j, P * i:P * i + P])
                if d >= 18:
                    weighted(d - 2)
                if 17 <= d <= 32:
                    transposes(d - 1)
                for j in {31: (0,), 32: (1, 2)}.get(d, ()):
                    pe.wait_ge(s_y, 16 + 4 * j + 4)
                    batch(yg_batch(j), lambda i: ytok[:, j, P * i:P * i + P])
            pe.wait_ge(s_y, 32)
            batch(yg_batch(3), lambda i: ytok[:, 3, P * i:P * i + P])
            batches_out(B_X2)
            pe.wait_ge(s_p, 64)
            pe.wait_ge(s_ht, KD + 4)
            for b in range(KD):
                pe.wait_ge(s_lo, P_BR + b + 1)
                if b >= 2:
                    pe.wait_ge(s_bread, b - 1)
                w = weights(P_BR + b, KD)
                for k in range(KD):
                    last = split_mm(ps[:, 2 * (b % 2) + k // 4, :], cut(w, k, 0, P), acts(k), k % 4 == 0, k % 4 == 3)
                last.then_inc(s_pused, 1)

            def h2_transposes(j):
                pe.wait_ge(s_xh2, j + 1)
                for i in range(2):
                    batch(B_X2 + 2 * j + i, lambda k: xh2[:, j, P * (4 * i + k):P * (4 * i + k) + P])

            def logits(j):
                batches_out(B_X2 + 2 * j + 2)
                for k in range(KD):
                    last = mm(ps[:, 3, E * j:E * j + E], h2t[:, k, P * j:P * j + P], wr[:, k, :], start=(k == 0),
                              stop=(k == KD - 1))
                return last

            pe.wait_ge(s_bread, KD)
            pe.wait_ge(s_bc, 3)
            for t in range(2):
                for k, j in [(k, 2 * t + i) for k in range(KD) for i in range(2)]:
                    p = P_OUT + KD * t + k
                    if j % 2 == 0:
                        pe.wait_ge(s_lo, p + 1)
                        if t == 0:
                            pe.wait_ge(s_ht, KD + 4 + k + 1)
                    if j == 3 and k == 0:
                        pe.wait_ge(s_oread, 1)
                    w = weights(p, 1)
                    for h in range(2):
                        last = split_mm(ps[:, (0, 2, 6, 0)[j] + h, :], acts(k, P * j, P * j + P),
                                        cut(w, 0, 512 * h, 512 * h + 512), k == 0, k == KD - 1)
                    if j % 2:
                        last.then_inc(s_pused, 1)
                    elif k == KD - 1:
                        last.then_inc(s_op, 1)
                    if (j, k) == (3, 5):
                        h2_transposes(0)
            pe.wait_ge(s_opout, 2)
            h2_transposes(1)
            logits(0)
            keep_clock(3, 2, xh2[:, 0, 0:512])
            h2_transposes(2)
            logits(1)
            h2_transposes(3)
            logits(2)
            logits(3).then_inc(s_log, 1)
            pe.wait_ge(s_aff, 1)
            bank_free(B_AFF)
            for j in range(NT):
                last = nc.tensor.transpose(ps[0:E, 4 + B_AFF % 2, P * j:P * j + P], aff[:, j, :], ident)
            last.then_inc(s_tdone, 1)
            keep_clock(14, 2, xh2[:, 0, 0:512])
            pe.wait_ge(s_slot, 1)
            bank_free(B_SLOT)
            for j in range(NT):
                last = nc.tensor.transpose(ps[:, 4 + B_SLOT % 2, E * j:E * j + E], slot_e[:, P * j:P * j + P],
                                           ident[0:E, 0:E])
            last.then_inc(s_tdone, 1)

            keep_clock(1, 2, xh2[:, 0, 0:512])
            def tile_in(group, q, i):
                n = ET * q + i
                pe.wait_ge(s_e[eslot(n)], group * (16 * GROUP * ET // E_SLOTS) + 16 * (n // E_SLOTS + 1))
                return e_tile(eslot(n))

            def expert(group, q, last_one=False):
                e = group * GROUP + q
                pe.wait_ge(s_pick, e + 1)
                for j in range(NT):
                    for h in range(2):
                        last = mm(ps[64 * h:64 * h + 64, 7, :], pick[:, j, :], xh2[:, j, 512 * h:512 * h + 512],
                                  start=(j == 0), stop=(j == NT - 1), skip_group_check=True)
                last.then_inc(s_gath, 1)
                pe.wait_ge(s_gready, e + 1)
                for j in range(NT):
                    last = nc.tensor.transpose(ps[:, 6, P * j:P * j + P], give[:, j, :], ident)
                last.then_inc(s_give, 1)
                pe.wait_ge(s_xin, e + 1)
                for b in range(4):
                    last = nc.tensor.transpose(ps[:, 5, P * b:P * b + P], xin[:, P * b:P * b + P], ident)
                last.then_inc(s_xt, 1)
                pe.wait_ge(s_cbout, e * NT + 1)
                for g in range(2):
                    for up in range(2):
                        for k2 in range(4):
                            w = tile_in(group, q, 8 * g + 4 * up + k2)
                            if g + up == 0:
                                pe.wait_ge(s_xinT, e * KD + (2 * k2 + 2))
                            for kk in range(2):
                                for h in range(2):
                                    last = mm(ps[64 * h:64 * h + 64, 2 * g + up, :], xinT[:, 2 * k2 + kk, :],
                                              w[:, kk, 512 * h:512 * h + 512], start=(k2 + kk == 0),
                                              stop=(k2 + kk == 4), skip_group_check=True)
                            last.then_inc(s_wused, 1)
                for g in range(2):
                    pe.wait_ge(s_act, 2 * e + (g + 1))
                    if g:
                        pe.wait_ge(s_giveT, e + 1)
                    for b in range(4):
                        last = nc.tensor.transpose(ps[:, 5 + g, P * b:P * b + P], act[:, g, P * b:P * b + P], ident)
                    last.then_inc(s_at, 1)
                for i in range(8):
                    if i % 4 == 0:
                        pe.wait_ge(s_actT, 2 * e + (i // 4 + 1))
                    if last_one and i >= 3:
                        keep_clock(1, 7, xh2[:, 0, 0:512])
                    w = tile_in(group, q, 16 + i)
                    for kk in range(2):
                        f = 2 * i + kk
                        for h in range(2):
                            last = mm(ps[64 * h:64 * h + 64, 4, :], actT[:, f, :], w[:, kk, 512 * h:512 * h + 512],
                                      start=(f == 0), stop=(f == 15), skip_group_check=True)
                    last.then_inc(s_wused, 1)
                if last_one:
                    keep_clock(1, 7, xh2[:, 0, 0:512])
                pe.wait_ge(s_ysb, e + 1)
                for j in range(NT):
                    if j >= 2:
                        pe.wait_ge(s_cbout, e * NT + j)
                    for h in range(2):
                        last = mm(ps[:, 2 * (j % 2) + h, :], giveT[64 * h:64 * h + 64, P * j:P * j + P],
                                  ysb[64 * h:64 * h + 64, :], start=True, stop=True)
                    last.then_inc(s_cb, 1)

            with pe.Fori(0, E // GROUP) as group:
                for q in range(GROUP):
                    expert(group, q)
            for q in range(E % GROUP):
                expert(E // GROUP, q, last_one=(q == E % GROUP - 1))



_INS = ['x', 'c', 'w_ada', 'b_ada', 'norm1_g', 'w_in', 'q_norm_g', 'k_norm_g', 'na_rpb', 'w_branch_na', 'w_branch_gqa',
        'w_out', 'norm2_g', 'w_router', 'w_exp_gate', 'w_exp_up', 'w_exp_down', 'final_g']
_STACKED = {'w_ada', 'w_in', 'w_branch_na', 'w_branch_gqa', 'w_out', 'w_router', 'w_exp_gate', 'w_exp_up', 'w_exp_down'}


def _constants(np):
    cols, rows, hd = 64, 8, 64
    out = np.zeros((128, 4 * 128 + 768), np.float32)
    out[:, 0:128] = np.eye(128)
    out[:, 128:256] = np.arange(128) % 64 + 1
    half = hd // 2
    inv = np.float32(10000.0) ** (-np.arange(0, half, 2, dtype=np.float32) / np.float32(half))
    t = np.arange(cols * rows)
    col, row = (t // rows).astype(np.float32), (t % rows).astype(np.float32)
    ang = np.concatenate([row[:, None] * inv[None], col[:, None] * inv[None]], axis=-1).astype(np.float32)
    for i, f in ((256, np.cos), (384, np.sin)):
        out[:, i:i + 128] = f(ang).reshape(4, 128, half).transpose(1, 0, 2).reshape(128, 128)
    for v, (c0, k0) in enumerate(((16, 8), (0, 0), (48, 40))):
        q = c0 + np.arange(128) // rows
        start = np.clip(q - 8, 0, cols - 16)
        k = k0 + np.arange(256) // rows
        ok = (k[None] >= start[:, None]) & (k[None] < start[:, None] + 16)
        out[:, 512 + 256 * v:768 + 256 * v] = np.where(ok, 0.0, -1e30)
    return out


def kernel(**inputs):
    import numpy as _np
    import concourse.bacc as _bacc
    from concourse import mybir as _mybir
    from concourse.bass_utils import run_bass_kernel_spmd as _run

    nc = _bacc.Bacc("TRN2", target_bir_lowering=False, num_devices=1)
    arrays, args = {}, []
    for name in _INS + ['consts']:
        a = _constants(_np) if name == 'consts' else _np.asarray(inputs[name])
        if name in _STACKED:
            a = a.reshape(a.shape[1:])
        if name == 'na_rpb':
            a = _np.pad(a[0][:, ::-1].transpose(1, 0, 2), ((0, 0), (0, 0), (8, 8)))
        a = _np.ascontiguousarray(a)
        arrays[f"in_{name}"] = a
        args.append(nc.dram_tensor(f"in_{name}", a.shape, _mybir.dt.from_np(a.dtype), kind="ExternalInput").ap())
    out = nc.dram_tensor("out_0", inputs['x'].shape, _mybir.dt.float32, kind="ExternalOutput").ap()
    encoder_block(nc, *args, out)
    r = _run(nc, [arrays], core_ids=[0])
    return r.results[0]["out_0"]
```
